# Optimizing a Trainium2 kernel written in Bass

```python
import jax, jax.numpy as jnp
from jax import lax
import numpy as np

D_MODEL = 1024
BATCH = 1
SEQ = 2048
DEPTH = 1

CTX_LEN = 256
GRID_W = 64
EXPAND = 2
MIX_WIDTH = EXPAND * D_MODEL
HGRN_WIDTH = MIX_WIDTH // 2
FOURIER_WIDTH = MIX_WIDTH - HGRN_WIDTH
HGRN_HEAD_DIM = 128
HGRN_HEADS = HGRN_WIDTH // HGRN_HEAD_DIM
FOURIER_GROUPS = 4
FOURIER_GROUP_DIM = FOURIER_WIDTH // FOURIER_GROUPS
IN_WIDTH = 5 * HGRN_WIDTH + 2 * FOURIER_WIDTH
CHUNK = 32
POS_BASE = 10000.0
EPS = 1e-6
F_MIN = 1e-6

kernel_name = "hybrid_hgrn2_fnet_prefix"

F32 = jnp.float32

def rmsnorm(x, w):
    xf = x.astype(F32)
    y = xf * lax.rsqrt(jnp.mean(xf * xf, axis=-1, keepdims=True) + EPS)
    return (y * w.astype(F32)).astype(x.dtype)

def sincos_2d(length, dim):
    rows = length // GRID_W
    row = jnp.repeat(jnp.arange(rows, dtype=F32), GRID_W)
    col = jnp.tile(jnp.arange(GRID_W, dtype=F32), rows)
    quarter = dim // 4
    omega = jnp.power(POS_BASE, -jnp.arange(quarter, dtype=F32) / quarter)

    def axis_code(p):
        ang = p[:, None] * omega[None, :]
        return jnp.concatenate([jnp.sin(ang), jnp.cos(ang)], axis=-1)

    return jnp.concatenate([axis_code(row), axis_code(col)], axis=-1)

def to_heads(t):
    return t.reshape(t.shape[:-1] + (HGRN_HEADS, HGRN_HEAD_DIM))

def split_proj(p):
    a = HGRN_WIDTH
    return jnp.split(p, [a, 2 * a, 3 * a, 4 * a, 5 * a, 5 * a + FOURIER_WIDTH], axis=-1)

def layer_lower_bounds(lower_bounds):
    p = jax.nn.softmax(lower_bounds.astype(F32), axis=1)
    return jnp.cumsum(p, axis=1) - p[:, :1]

def forget_gate(z, lb):
    z = z.astype(F32)
    lb = lb.reshape(HGRN_HEADS, HGRN_HEAD_DIM)
    k = (1.0 - lb) * jax.nn.sigmoid(-z)
    log_f = jnp.log(jnp.maximum(1.0 - k, F_MIN))
    return k, log_f

def chunk_scan(q, k, v, log_f, s0):
    b_, length, h, _ = q.shape
    dv = v.shape[-1]
    n = length // CHUNK

    def blocks(t):
        return t.reshape(b_, n, CHUNK, h, t.shape[-1]).transpose(1, 0, 3, 2, 4)

    tri = jnp.tril(jnp.ones((CHUNK, CHUNK), dtype=bool))[:, :, None]

    def step(state, inp):
        qc, kc, vc, gc = inp
        bcum = jnp.cumsum(gc, axis=2)
        o_inter = jnp.einsum("bhtd,bhde->bhte", qc * jnp.exp(bcum), state)
        rel = jnp.where(tri, bcum[:, :, :, None, :] - bcum[:, :, None, :, :], 0.0)
        decay = jnp.where(tri, jnp.exp(rel), 0.0)
        scores = jnp.einsum("bhtd,bhsd,bhtsd->bhts", qc, kc, decay)
        o_intra = jnp.einsum("bhts,bhse->bhte", scores, vc)
        b_end = bcum[:, :, -1:, :]
        state = state * jnp.exp(b_end)[:, :, 0, :, None] + jnp.einsum(
            "bhsd,bhse->bhde", kc * jnp.exp(b_end - bcum), vc)
        return state, o_inter + o_intra

    s_final, o = lax.scan(step, s0, (blocks(q), blocks(k), blocks(v), blocks(log_f)))
    return o.transpose(1, 0, 3, 2, 4).reshape(b_, length, h, dv), s_final

def final_state(k, v, log_f):
    bcum = jnp.cumsum(log_f, axis=1)
    w = k * jnp.exp(bcum[:, -1:] - bcum)
    return jnp.einsum("bthd,bthe->bhde", w, v)

def fourier_mix(u, w_four, b_four):
    b_, length, _ = u.shape
    ug = u.astype(F32).reshape(b_, length, FOURIER_GROUPS, FOURIER_GROUP_DIM)
    spec = jnp.fft.fftn(ug, axes=(1, 3), norm="ortho").real
    y = jnp.einsum("blgc,gcd->blgd", spec, w_four.astype(F32)).reshape(b_, length, FOURIER_WIDTH)
    return (y + b_four.astype(F32)).astype(u.dtype)

def mix_stream(h, w_in, lb_f, lb_b, s0_f, s0_b, hn_w, w_four, b_four, w_out):
    p = h @ w_in
    i_in, z_f, z_b, q_in, gate_a, u_f, gate_f = split_proj(p)
    v = to_heads(i_in).astype(F32)
    q = jax.nn.silu(to_heads(q_in).astype(F32))
    k_f, g_f = forget_gate(to_heads(z_f), lb_f)
    k_b, g_b = forget_gate(to_heads(z_b), lb_b)
    o_f, s_f = chunk_scan(q, k_f, v, g_f, s0_f)
    flip = lambda t: jnp.flip(t, axis=1)
    o_b, s_b = chunk_scan(flip(q), flip(k_b), flip(v), flip(g_b), s0_b)
    o = o_f + flip(o_b)
    o = o * lax.rsqrt(jnp.mean(o * o, axis=-1, keepdims=True) + EPS)
    o = o * hn_w.astype(F32).reshape(HGRN_HEADS, HGRN_HEAD_DIM)
    y_a = o.reshape(h.shape[:-1] + (HGRN_WIDTH,)).astype(h.dtype) * jax.nn.silu(gate_a)
    y_f = fourier_mix(u_f, w_four, b_four) * jax.nn.silu(gate_f)
    out = jnp.concatenate([y_a, y_f], axis=-1) @ w_out
    return out, s_f, s_b

def context_final_states(h, w_in, lb_f, lb_b):
    p = h @ w_in[:, :3 * HGRN_WIDTH]
    i_in, z_f, z_b = jnp.split(p, [HGRN_WIDTH, 2 * HGRN_WIDTH], axis=-1)
    v = to_heads(i_in).astype(F32)
    k_f, g_f = forget_gate(to_heads(z_f), lb_f)
    k_b, g_b = forget_gate(to_heads(z_b), lb_b)
    flip = lambda t: jnp.flip(t, axis=1)
    return final_state(k_f, v, g_f), final_state(flip(k_b), flip(v), flip(g_b))

def setup_inputs(seed: int = 0) -> dict:
    key = jax.random.key(seed)
    ks = jax.random.split(key, 14)
    d = D_MODEL
    nrm = lambda k, s: jax.random.normal(k, s, dtype=F32)
    return {
        "x": nrm(ks[0], (BATCH, SEQ, d)),
        "c": nrm(ks[1], (BATCH, d)),
        "ctx": nrm(ks[2], (BATCH, CTX_LEN, d)),
        "c_ctx": nrm(ks[3], (d,)),
        "norm_w": 1.0 + 0.02 * nrm(ks[4], (DEPTH, d)),
        "w_ada": 0.5 * d ** -0.5 * nrm(ks[5], (DEPTH, d, 3 * d)),
        "b_ada": 0.01 * nrm(ks[6], (DEPTH, 3 * d)),
        "w_in": d ** -0.5 * nrm(ks[7], (DEPTH, d, IN_WIDTH)),
        "lower_bounds": 1.0 + 0.1 * nrm(ks[8], (2, DEPTH, HGRN_WIDTH)),
        "hgrn_norm_w": 1.0 + 0.02 * nrm(ks[9], (DEPTH, HGRN_WIDTH)),
        "w_fourier": FOURIER_GROUP_DIM ** -0.5 * nrm(ks[10], (DEPTH, FOURIER_GROUPS, FOURIER_GROUP_DIM, FOURIER_GROUP_DIM)),
        "b_fourier": 0.01 * nrm(ks[11], (DEPTH, FOURIER_WIDTH)),
        "w_out": MIX_WIDTH ** -0.5 * nrm(ks[12], (DEPTH, MIX_WIDTH, d)),
        "final_norm_w": 1.0 + 0.02 * nrm(ks[13], (d,)),
    }

def reference(x, c, ctx, c_ctx, norm_w, w_ada, b_ada, w_in, lower_bounds, hgrn_norm_w,
              w_fourier, b_fourier, w_out, final_norm_w):
    b_, length, d = x.shape
    x = x + sincos_2d(length, d).astype(x.dtype)[None]
    lbs = layer_lower_bounds(lower_bounds)
    sc = jax.nn.silu(c)
    scc = jax.nn.silu(c_ctx)
    zero = jnp.zeros((b_, HGRN_HEADS, HGRN_HEAD_DIM, HGRN_HEAD_DIM), dtype=F32)
    for l in range(DEPTH):
        shift, scale, gate = jnp.split(sc @ w_ada[l] + b_ada[l], 3, axis=-1)
        shift_c, scale_c, gate_c = jnp.split(scc @ w_ada[l] + b_ada[l], 3, axis=-1)
        hc = rmsnorm(ctx, norm_w[l]) * (1.0 + scale_c) + shift_c
        if l < DEPTH - 1:
            out_c, s_f, s_b = mix_stream(hc, w_in[l], lbs[0, l], lbs[1, l], zero, zero,
                                         hgrn_norm_w[l], w_fourier[l], b_fourier[l], w_out[l])
        else:
            s_f, s_b = context_final_states(hc, w_in[l], lbs[0, l], lbs[1, l])
        hx = rmsnorm(x, norm_w[l]) * (1.0 + scale[:, None]) + shift[:, None]
        out_x, _, _ = mix_stream(hx, w_in[l], lbs[0, l], lbs[1, l], s_f, s_b,
                                 hgrn_norm_w[l], w_fourier[l], b_fourier[l], w_out[l])
        x = x + gate[:, None] * out_x
        if l < DEPTH - 1:
            ctx = ctx + gate_c * out_c
    return rmsnorm(x, final_norm_w)


_drawn_inputs = setup_inputs


def setup_inputs(seed=0):
    import zlib

    import numpy as np

    out = dict(_drawn_inputs(seed))
    spreads = {}
    factors = {'ctx': 51.148,
     'c_ctx': 64.0,
     'norm_w': 8.0,
     'b_ada': 8.0,
     'hgrn_norm_w': 27.864,
     'b_fourier': 51.017,
     'final_norm_w': 7.815}
    for name, (base, spread) in spreads.items():
        noise = np.random.default_rng([zlib.crc32(name.encode()), seed]).standard_normal(out[name].shape)
        drawn = base * np.exp(spread * noise) if base else spread * noise
        out[name] = __import__('jax').numpy.asarray(drawn.astype(out[name].dtype))
    for name, factor in factors.items():
        out[name] = (out[name] * factor).astype(out[name].dtype)
    return out
```

```python
from contextlib import ExitStack

import concourse.bass as bass
import numpy as np
from concourse import mybir
from concourse.alu_op_type import AluOpType as ALU

F32 = mybir.dt.float32
F32R = mybir.dt.float32r
U8 = mybir.dt.uint8
ACT = mybir.ActivationFunctionType
AX = mybir.AxisListType

P = 128
D = 1024
SEQ = 2048
CTX = 256
GRID_W = 64
KT = D // P
HEADS = 8
HG = HEADS * P
FG = 4
FC = 256
FW = FG * FC
MIX = HG + FW
NT = SEQ // P
GRP = 512
NG = SEQ // GRP
TPG = GRP // P
EPS = 1e-6
F_MIN = 1e-6
COL_I, COL_ZF, COL_ZB, COL_Q, COL_GA, COL_U, COL_GF = (HG * 0, HG, 2 * HG, 3 * HG, 4 * HG, 5 * HG, 5 * HG + FW)
DMA = 16


def mm3(nc, out, st_hi, st_lo, mv_hi, mv_lo, start, stop):
    nc.tensor.matmul(out, st_hi, mv_hi, start=start, stop=False)
    nc.tensor.matmul(out, st_hi, mv_lo, start=False, stop=False)
    return nc.tensor.matmul(out, st_lo, mv_hi, start=False, stop=stop)


def after(engine, sem, n):
    engine.wait_ge(sem, n + 1)


def row_on_all(ap_1d, n):
    return ap_1d.rearrange("(o n) -> o n", o=1).to_broadcast([P, n])


class Room:

    def __init__(self, nc, stage):
        self.nc, self.stage, self.stack, self.sems, self.at_one = nc, stage, ExitStack(), [], []

    def __enter__(self):
        return self

    def __exit__(self, failed, *a):
        if self.sems and not failed:
            with self.nc.Block() as block:

                @block.gpsimd
                def _(pool):
                    for s in self.sems:
                        pool.sem_clear(s)
        self.stack.close()

    def sb(self, name, shape, dt=F32):
        return self.stack.enter_context(self.nc.sbuf_tensor(f"{self.stage}_{name}", shape, dt))

    def ps(self, name, shape=(P, GRP), dt=F32):
        return self.stack.enter_context(self.nc.psum_tensor(f"{self.stage}_{name}", list(shape), dt))

    def sem(self, name, from_zero=False):
        s = self.stack.enter_context(self.nc.semaphore(f"{self.stage}_{name}"))
        self.sems.append(s)
        if not from_zero:
            self.at_one.append(s)
        return s

    def start_at_one(self):
        with self.nc.Block() as block:

            @block.gpsimd
            def _(pool):
                for s in self.at_one:
                    pool.sem_inc(s, 1)




def constants(nc, masks_in, ident, masks):
    with Room(nc, "const") as r:
        wide = r.sb("wide", [P, 2, MASKED, P])
        cleared, ident_done, masks_here, masks_done = (r.sem(n) for n in ("cleared", "ident_done", "masks_here", "masks_done"))
        with nc.Block() as block:

            @block.sync
            def _(sp):
                sp.dma_start(wide[:], masks_in).then_inc(masks_here, DMA)

            @block.gpsimd
            def _(pool):
                pool.memset(ident[:], 0.0).then_inc(cleared, 1)
                pool.wait_ge(cleared, 1)
                pool.affine_select(out=ident[:], in_=ident[:], compare_op=ALU.not_equal, fill=1.0, base=0,
                                   pattern=[[-1, P]], channel_multiplier=1).then_inc(ident_done, 1)

            @block.vector
            def _(v):
                v.wait_ge(masks_here, DMA)
                nc.vector.tensor_copy(masks[:], wide[:]).then_inc(masks_done, 1)


def modulation(nc, conds, w_ada, b_ada, b_ada_cols, norm_w_cols, bounds_cols, mod_mul, mod_add, one_minus_lb, gate_rows):
    AB = 3 * D // GRP
    GB = 2 * D // GRP
    with Room(nc, "mod") as r:
        cond = r.sb("cond", [P, KT, 2])
        silu = r.sb("silu", [P, KT, 2])
        silu_rows = r.sb("silu_rows", [P, KT, P])
        w = [r.sb(f"w{i}", [P, KT, GRP]) for i in range(AB)]
        bias = r.sb("bias", [P, 2 * KT])
        gate_bias = r.sb("gate_bias", [P, D])
        nw = r.sb("nw", [P, KT])
        vec = r.sb("vec", [P, 2 * KT, 2])
        gate = r.sb("gate", [P, D])
        lb_in = r.sb("lb_in", [P, 2, HEADS])
        lb_exp = r.sb("lb_exp", [P, 2, HEADS])
        lb_inv = r.sb("lb_inv", [P, 2, HEADS])
        lb = r.sb("lb", [P, 2, HEADS])
        ps_vec = r.ps("ps_vec", [P, 2 * KT, 2])
        ps_gate = [r.ps(f"ps_gate{i}") for i in range(2)]
        cond_in, small_in, silu_done, rows_done = r.sem("cond_in"), r.sem("small_in"), r.sem("silu_done"), r.sem("rows_done")
        w_in_sem = [r.sem(f"w_in{i}") for i in range(AB)]
        vec_done, gate_done, dve, exp_done, gate_out = r.sem("vec_done"), r.sem("gate_done"), r.sem("dve"), r.sem("exp_done"), r.sem("gate_out")
        w_view = w_ada[0].rearrange("(k p) n -> p k n", p=P)
        with nc.Block() as block:

            @block.sync
            def _(sp):
                sp.dma_start(cond[:], conds).then_inc(cond_in, DMA)
                for i in range(AB):
                    sp.dma_start(w[i][:], w_view[:, :, i * GRP:(i + 1) * GRP]).then_inc(w_in_sem[i], DMA)
                sp.wait_ge(dve, 9)
                sp.dma_start(gate_rows, gate[:]).then_inc(gate_out, DMA)
                sp.wait_ge(gate_out, DMA)

            @block.scalar
            def _(act):
                act.dma_start(bias[:], b_ada_cols[:, 0:2 * KT]).then_inc(small_in, DMA)
                act.dma_start(gate_bias[:], row_on_all(b_ada[0, 2 * D:3 * D], D)).then_inc(small_in, DMA)
                act.dma_start(nw[:], norm_w_cols).then_inc(small_in, DMA)
                act.dma_start(lb_in[:], bounds_cols).then_inc(small_in, DMA)
                act.wait_ge(cond_in, DMA)
                nc.scalar.activation(silu[:], cond[:], ACT.Silu).then_inc(silu_done, 1)
                act.wait_ge(dve, 1)
                nc.scalar.activation(lb_exp[:], lb_exp[:], ACT.Exp).then_inc(exp_done, 1)

            @block.tensor
            def _(pe):
                pe.wait_ge(silu_done, 1)
                for b in range(GB):
                    pe.wait_ge(w_in_sem[b], DMA)
                    for m in range(GRP // P):
                        for k in range(KT):
                            last = nc.tensor.matmul(ps_vec[:, b * (GRP // P) + m, :], w[b][:, k, m * P:(m + 1) * P],
                                                    silu[:, k, :], start=k == 0, stop=k == KT - 1)
                last.then_inc(vec_done, 1)
                pe.wait_ge(rows_done, 1)
                for b in range(GB, AB):
                    pe.wait_ge(w_in_sem[b], DMA)
                    for k in range(KT):
                        last = nc.tensor.matmul(ps_gate[b - GB][:], silu_rows[:, k, :], w[b][:, k, :],
                                                start=k == 0, stop=k == KT - 1)
                    last.then_inc(gate_done, 1)

            @block.vector
            def _(v):
                v.wait_ge(small_in, 4 * DMA)
                nc.vector.tensor_tensor(lb_exp[:], lb_in[:], lb_in[:], ALU.subtract).then_inc(dve, 1)
                v.wait_ge(silu_done, 1)
                nc.vector.tensor_copy(silu_rows[:], silu[:, :, 0:1].to_broadcast([P, KT, P])).then_inc(rows_done, 1)
                v.wait_ge(exp_done, 1)
                nc.vector.reciprocal(lb_inv[:], lb_exp[:]).then_inc(dve, 1)
                v.wait_ge(dve, 2)
                nc.vector.tensor_tensor(lb[:], lb_exp[:], lb_inv[:], ALU.mult).then_inc(dve, 1)
                v.wait_ge(dve, 3)
                nc.vector.tensor_tensor(lb_inv[:], lb[:], lb[:], ALU.subtract).then_inc(dve, 1)
                v.wait_ge(dve, 4)
                nc.vector.tensor_scalar(one_minus_lb[:], lb_inv[:], -1.0, 1.0, ALU.mult, ALU.add).then_inc(dve, 1)
                v.wait_ge(vec_done, 1)
                nc.vector.tensor_tensor(vec[:], ps_vec[:], bias[:].rearrange("p (n o) -> p n o", o=1).to_broadcast([P, 2 * KT, 2]),
                                        ALU.add).then_inc(dve, 1)
                v.wait_ge(dve, 6)
                nc.vector.tensor_copy(mod_add[:], vec[:, 0:KT, :])
                nc.vector.scalar_tensor_tensor(mod_mul[:], vec[:, KT:2 * KT, :], 1.0,
                                               nw[:].rearrange("p (n o) -> p n o", o=1).to_broadcast([P, KT, 2]),
                                               ALU.add, ALU.mult).then_inc(dve, 1)
                for i in range(2):
                    v.wait_ge(gate_done, i + 1)
                    nc.vector.tensor_tensor(gate[:, i * GRP:(i + 1) * GRP], ps_gate[i][:],
                                            gate_bias[:, i * GRP:(i + 1) * GRP], ALU.add).then_inc(dve, 1)


def hidden(nc, stage, src, tiles, stream, row_code, col_code, mod_mul, mod_add, ident, h_hi, h_lo):
    coded = row_code is not None
    H = D // 2
    RING = min(4, tiles)
    TURNS = tiles // RING
    LOADS = 1 + P // GRID_W if coded else 1
    with Room(nc, stage) as r:
        x = [r.sb(f"x{b}", [P, D]) for b in range(RING)]
        row = [r.sb(f"row{b}", [P, H]) for b in range(RING)] if coded else None
        col = r.sb("col", [P, H]) if coded else None
        square = r.sb("square", [P, D])
        h = [r.sb(f"h{b}", [P, KT, P]) for b in range(2)]
        eps = r.sb("eps", [P, 1])
        warm = r.sb("warm", [P, 1])
        stat = [r.sb(f"stat{b}", [P, 3]) for b in range(RING)]
        ps = [[r.ps(f"ps{b}{i}", [P, KT // 2, P]) for i in range(2)] for b in range(2)]
        x_in = [r.sem(f"x_in{b}") for b in range(RING)]
        col_in, eps_set, warmed = r.sem("col_in"), r.sem("eps_set"), r.sem("warmed")
        coded_done, root_done, sq_done, normed = r.sem("coded_done"), r.sem("root_done"), r.sem("sq_done"), r.sem("normed")
        inv_done, turned, modulated, split_hi, split_done = (r.sem(n) for n in
                                                             ("inv_done", "turned", "modulated", "split_hi", "split_done"))

        def ahead(i, b):
            return i + b // RING, b % RING

        def staged_turn(i, last, first_stage, second_stage, third_stage):
            for b in range(RING):
                if not last or b + 2 < RING:
                    first_stage(*ahead(i, b + 2))
                if not last or b + 1 < RING:
                    second_stage(*ahead(i, b + 1))
                third_stage(i, b)

        def over_turns(engine, turn):
            if TURNS > 1:
                with engine.Fori(0, TURNS - 1) as i:
                    turn(i, False)
            turn(TURNS - 1, True)

        r.start_at_one()
        with nc.Block() as block:

            @block.sync
            def _(sp):
                def load(t, b):
                    sp.dma_start(x[b][:], src[bass.ds(t * P, P), :]).then_inc(x_in[b], DMA)
                    if coded:
                        for half in range(P // GRID_W):
                            sp.dma_start(row[b][half * GRID_W:(half + 1) * GRID_W, :],
                                         row_code[bass.ds(t * 2 + half, 1), :].to_broadcast([GRID_W, H])).then_inc(x_in[b], DMA)

                for b in range(RING):
                    load(b, b)
                    if coded and b == 0:
                        for half in range(P // GRID_W):
                            sp.dma_start(col[half * GRID_W:(half + 1) * GRID_W, :], col_code).then_inc(col_in, DMA)
                if TURNS > 1:
                    with sp.Fori(1, TURNS) as i:
                        for b in range(RING):
                            after(sp, turned, i * RING + b - RING + 1)
                            load(i * RING + b, b)

            @block.vector
            def _(v):
                def add_codes(i, b):
                    if coded:
                        after(v, x_in[b], (i + 1) * LOADS * DMA)
                        nc.vector.tensor_tensor(x[b][:, 0:H], x[b][:, 0:H], row[b][:], ALU.add)
                        nc.vector.tensor_tensor(x[b][:, H:D], x[b][:, H:D], col[:], ALU.add).then_inc(coded_done, 1)

                def norm(i, b):
                    t = i * RING + b
                    after(v, root_done, t + 1)
                    nc.vector.reciprocal(stat[b][:, 2:3], stat[b][:, 1:2]).then_inc(inv_done, 1)
                    after(v, inv_done, t + 1)
                    nc.vector.tensor_scalar(x[b][:], x[b][:], stat[b][:, 2:3], None, ALU.mult).then_inc(normed, 1)

                def split(i, b):
                    t = i * RING + b
                    at = bass.ds(t * P, P)
                    after(v, modulated, t + 1)
                    nc.vector.tensor_copy(h_hi[:, :, at], h[b % 2][:]).then_inc(split_hi, 1)
                    after(v, split_hi, t + 1)
                    nc.vector.tensor_tensor(h_lo[:, :, at], h[b % 2][:], h_hi[:, :, at].bitcast(F32), ALU.subtract).then_inc(split_done, 1)

                nc.vector.memset(eps[:], EPS).then_inc(eps_set, 1)
                if coded:
                    after(v, col_in, P // GRID_W * DMA)
                add_codes(0, 0)
                add_codes(0, 1)
                norm(0, 0)
                over_turns(v, lambda i, last: staged_turn(i, last, add_codes, norm, split))

            @block.scalar
            def _(act):
                def root(i, b):
                    t = i * RING + b
                    if coded:
                        after(act, coded_done, t + 1)
                    else:
                        after(act, x_in[b], (i + 1) * DMA)
                    after(act, sq_done, t)
                    nc.scalar.activation(square[:], x[b][:], ACT.Square, accum_out=stat[b][:, 0:1]).then_inc(sq_done, 1)
                    after(act, sq_done, t + 1)
                    nc.scalar.activation(stat[b][:, 1:2], stat[b][:, 0:1], ACT.Sqrt, scale=1.0 / D, bias=eps[:, 0:1]).then_inc(root_done, 1)

                def modulate(i, b):
                    t = i * RING + b
                    after(act, turned, t + 1)
                    if b >= 2:
                        after(act, split_done, t - 1)
                    else:
                        after(act, split_done, i * RING)
                    for k in range(KT):
                        last = nc.scalar.activation(h[b % 2][:, k, :], ps[b % 2][k // 4][:, k % 4, :], ACT.Identity,
                                                    scale=mod_mul[:, k, stream:stream + 1], bias=mod_add[:, k, stream:stream + 1])
                    last.then_inc(modulated, 1)

                def turn(i, last):
                    after(act, warmed, i)
                    nc.scalar.activation(warm[:], eps[:], ACT.Sqrt).then_inc(warmed, 1)
                    staged_turn(i, last, lambda i, b: None, root, modulate)

                after(act, eps_set, 1)
                root(0, 0)
                over_turns(act, turn)

            @block.tensor
            def _(pe):
                def transpose(i, b):
                    t = i * RING + b
                    after(pe, normed, t + 1)
                    if b >= 2:
                        after(pe, modulated, t - 1)
                    else:
                        after(pe, modulated, i * RING)
                    for k in range(KT):
                        last = nc.tensor.transpose(ps[b % 2][k // 4][:, k % 4, :], x[b][:, k * P:(k + 1) * P], ident[:])
                    last.then_inc(turned, 1)

                over_turns(pe, lambda i, last: [transpose(i, b) for b in range(RING)])


def context(nc, w_in, one_minus_lb, ident, h_hi, h_lo, states):
    CT = CTX // P
    TURNS = HEADS // 2
    with Room(nc, "ctx") as r:
        def two(name, shape, dt=F32):
            return [r.sb(f"{name}{s}", shape, dt) for s in range(2)]

        def two_by_direction(name, shape):
            return [[r.sb(f"{name}{s}{d}", shape) for d in range(2)] for s in range(2)]

        raw = [[r.sb(f"raw{s}{j}", [P, KT, P]) for j in range(3)] for s in range(2)]
        hi = [[r.sb(f"hi{s}{j}", [P, KT, P], F32R) for j in range(3)] for s in range(2)]
        lo = [[r.sb(f"lo{s}{j}", [P, KT, P], F32R) for j in range(3)] for s in range(2)]
        value, state = two("value", [P, CT, P]), two("state", [P, 2, P])
        key, gate, suffix = two_by_direction("key", [P, CTX]), two_by_direction("gate", [P, CTX]), two_by_direction("suffix", [P, CTX])
        key_t = two_by_direction("key_t", [P, CT, P])
        ones = r.sb("ones", [P, CTX])
        ps_v = [r.ps(f"ps_v{s}", [P, CT, P]) for s in range(2)]
        ps_z = [r.ps(f"ps_z{d}", [P, CTX]) for d in range(2)]
        ps_kt = [r.ps(f"ps_kt{d}", [P, CT, P]) for d in range(2)]
        ps_s = r.ps("ps_s", [P, 2, P])
        w_here = [[r.sem(f"w_here{s}{j}") for j in range(3)] for s in range(2)]
        lo_done = [r.sem(f"lo_done{s}") for s in range(2)]
        s_out = [r.sem(f"s_out{s}") for s in range(2)]
        hi_done, set_once, v_done, z_done = (r.sem(n) for n in ("hi_done", "set_once", "v_done", "z_done"))
        v_copied, sig_done, gate_raw, key_done, scan_done, weighed = (r.sem(n) for n in
                                                            ("v_copied", "sig_done", "gate_raw", "key_done", "scan_done", "weighed"))
        turned, turned_copied, s_done, s_copied = (r.sem(n) for n in ("turned", "turned_copied", "s_done", "s_copied"))
        w_view = w_in[0].rearrange("(k p) n -> p k n", p=P)
        cols = (COL_I, COL_ZF, COL_ZB)
        r.start_at_one()
        with nc.Block() as block:

            @block.sync
            def _(sp):
                def load(i, s):
                    for j in range(3):
                        after(sp, lo_done[s], 3 * i)
                        sp.dma_start(raw[s][j][:], w_view[:, :, bass.ds((2 * i + s) * P + cols[j], P)]).then_inc(w_here[s][j], DMA)

                with sp.Fori(0, TURNS) as i:
                    load(i, 0)
                    load(i, 1)

            @block.scalar
            def _(act):
                def split_high(i, s):
                    for j in range(3):
                        after(act, w_here[s][j], (i + 1) * DMA)
                        nc.scalar.activation(hi[s][j][:], raw[s][j][:], ACT.Copy).then_inc(hi_done, 1)

                def leave_banks(i, s):
                    h = 2 * i + s
                    for d in range(2):
                        after(act, z_done, 2 * h + d + 1)
                        nc.scalar.activation(key[s][d][:], ps_z[d][:], ACT.Sigmoid, scale=-1.0).then_inc(sig_done, 1)
                    nc.scalar.activation(value[s][:], ps_v[s][:], ACT.Copy).then_inc(v_copied, 1)

                def finish(i, s):
                    h = 2 * i + s
                    for d in range(2):
                        after(act, turned, 2 * h + d + 1)
                        nc.scalar.activation(key_t[s][d][:], ps_kt[d][:], ACT.Copy).then_inc(turned_copied, 1)
                    after(act, s_done, h + 1)
                    after(act, s_out[s], i * 2 * DMA)
                    nc.scalar.activation(state[s][:], ps_s[:], ACT.Copy).then_inc(s_copied, 1)
                    after(act, s_copied, h + 1)
                    for d in range(2):
                        act.dma_start(states[d][bass.ds(h * P, P), :], state[s][:, d, :]).then_inc(s_out[s], DMA)

                def turn(i, last):
                    leave_banks(i, 1)
                    if not last:
                        split_high(i + 1, 0)
                    finish(i, 0)
                    if not last:
                        leave_banks(i + 1, 0)
                        split_high(i + 1, 1)
                    finish(i, 1)

                split_high(0, 0)
                split_high(0, 1)
                leave_banks(0, 0)
                with act.Fori(0, TURNS - 1) as i:
                    turn(i, False)
                turn(TURNS - 1, True)
                for s in range(2):
                    after(act, s_out[s], TURNS * 2 * DMA)

            @block.tensor
            def _(pe):
                def project(i, s):
                    h = 2 * i + s
                    after(pe, lo_done[s], 3 * i + 1)
                    for t in range(CT):
                        for k in range(KT):
                            last = mm3(nc, ps_v[s][:, t, :], h_hi[:, k, t * P:(t + 1) * P], h_lo[:, k, t * P:(t + 1) * P],
                                       hi[s][0][:, k, :], lo[s][0][:, k, :], k == 0, k == KT - 1)
                    last.then_inc(v_done, 1)
                    for d in range(2):
                        after(pe, lo_done[s], 3 * i + d + 2)
                        after(pe, sig_done, 2 * h)
                        for k in range(KT):
                            last = mm3(nc, ps_z[d][:], hi[s][d + 1][:, k, :], lo[s][d + 1][:, k, :], h_hi[:, k, :], h_lo[:, k, :],
                                       k == 0, k == KT - 1)
                        last.then_inc(z_done, 1)

                def finish(i, s):
                    h = 2 * i + s
                    for d in range(2):
                        after(pe, weighed, 2 * h + d + 1)
                        after(pe, turned_copied, 2 * h)
                        for t in range(CT):
                            last = nc.tensor.transpose(ps_kt[d][:, t, :], key[s][d][:, t * P:(t + 1) * P], ident[:])
                        last.then_inc(turned, 1)
                    after(pe, v_copied, h + 1)
                    after(pe, s_copied, h)
                    for d in range(2):
                        after(pe, turned_copied, 2 * h + d + 1)
                        for t in range(CT):
                            last = nc.tensor.matmul(ps_s[:, d, :], key_t[s][d][:, t, :], value[s][:, t, :], start=t == 0, stop=t == CT - 1)
                    last.then_inc(s_done, 1)

                def turn(i, last):
                    project(i, 1)
                    finish(i, 0)
                    if not last:
                        project(i + 1, 0)
                    finish(i, 1)

                project(0, 0)
                with pe.Fori(0, TURNS - 1) as i:
                    turn(i, False)
                turn(TURNS - 1, True)

            @block.vector
            def _(v):
                def split_low(i, s):
                    h = 2 * i + s
                    for j in range(3):
                        after(v, hi_done, 3 * h + j + 1)
                        nc.vector.tensor_tensor(lo[s][j][:], raw[s][j][:], hi[s][j][:].bitcast(F32), ALU.subtract).then_inc(lo_done[s], 1)

                def weigh(i, s):
                    h = 2 * i + s
                    for d in range(2):
                        after(v, sig_done, 2 * h + d + 1)
                        nc.vector.tensor_scalar(key[s][d][:], key[s][d][:], one_minus_lb[:, d, bass.ds(h, 1)], None,
                                                ALU.mult).then_inc(key_done, 1)
                    for d in range(2):
                        after(v, key_done, 2 * h + d + 1)
                        nc.vector.tensor_scalar(gate[s][d][:], key[s][d][:], -1.0, 1.0, ALU.mult, ALU.add).then_inc(gate_raw, 1)
                    for d in range(2):
                        after(v, gate_raw, 4 * h + d + 1)
                        nc.vector.tensor_scalar(gate[s][d][:], gate[s][d][:], F_MIN, None, ALU.max).then_inc(gate_raw, 1)
                    for d in range(2):
                        after(v, gate_raw, 4 * h + 3 + d)
                        if d == 0:
                            out, data = suffix[s][0][:, CTX - 2::-1], gate[s][0][:, CTX - 1:0:-1]
                        else:
                            out, data = suffix[s][1][:, 1:CTX], gate[s][1][:, 0:CTX - 1]
                        nc.vector.tensor_tensor_scan(out, data, ones[:, 0:CTX - 1], 1.0, ALU.mult, ALU.mult).then_inc(scan_done, 1)
                    for d in range(2):
                        after(v, scan_done, 2 * h + d + 1)
                        nc.vector.tensor_tensor(key[s][d][:], key[s][d][:], suffix[s][d][:], ALU.mult).then_inc(weighed, 1)

                def turn(i, last):
                    weigh(i, 1)
                    if not last:
                        split_low(i + 1, 0)
                        weigh(i + 1, 0)
                        split_low(i + 1, 1)

                nc.vector.memset(ones[:], 1.0).then_inc(set_once, 1)
                for s in range(2):
                    nc.vector.memset(suffix[s][0][:, CTX - 1:CTX], 1.0).then_inc(set_once, 1)
                    nc.vector.memset(suffix[s][1][:, 0:1], 1.0).then_inc(set_once, 1)
                after(v, set_once, 5)
                split_low(0, 0)
                split_low(0, 1)
                weigh(0, 0)
                with v.Fori(0, TURNS - 1) as i:
                    turn(i, False)
                turn(TURNS - 1, True)


def natural(nc, w_in, h_hi, h_lo, value_rows, gate_rows_a):
    W = 256
    STORE = 4
    TURNS = HG // W
    FILLS = NT // 2
    with Room(nc, "nat") as r:
        raw = [r.sb(f"raw{b}", [P, KT, W]) for b in range(2)]
        hi = [r.sb(f"hi{b}", [P, KT, W], F32R) for b in range(2)]
        lo = [r.sb(f"lo{b}", [P, KT, W], F32R) for b in range(2)]
        out = [r.sb(f"out{i}", [P, STORE, W]) for i in range(2)]
        ps = [[r.ps(f"ps{b}{i}", [P, 2, W]) for i in range(4)] for b in range(2)]
        w_here, hi_done, lo_done, product, evacuated = ([r.sem(f"{n}{b}") for b in range(2)] for n in
                                                        ("w_here", "hi_done", "lo_done", "product", "evacuated"))
        stored = [r.sem(f"stored{i}") for i in range(2)]
        w_view = w_in[0].rearrange("(k p) n -> p k n", p=P)
        cols, rows = (COL_I, COL_GA), [m.rearrange("(t p) n -> p t n", p=P) for m in (value_rows, gate_rows_a)]
        funcs = (ACT.Copy, ACT.Silu)
        r.start_at_one()
        with nc.Block() as block:

            @block.sync
            def _(sp):
                with sp.Fori(0, TURNS) as i:
                    for b in range(2):
                        after(sp, lo_done[b], i)
                        sp.dma_start(raw[b][:], w_view[:, :, bass.ds(i * W + cols[b], W)]).then_inc(w_here[b], DMA)

            @block.vector
            def _(v):
                with v.Fori(0, TURNS) as i:
                    for b in range(2):
                        after(v, w_here[b], (i + 1) * DMA)
                        after(v, product[b], i * FILLS)
                        nc.vector.tensor_copy(hi[b][:], raw[b][:]).then_inc(hi_done[b], 1)
                        after(v, hi_done[b], i + 1)
                        nc.vector.tensor_tensor(lo[b][:], raw[b][:], hi[b][:].bitcast(F32), ALU.subtract).then_inc(lo_done[b], 1)

            @block.tensor
            def _(pe):
                with pe.Fori(0, TURNS) as i:
                    for b in range(2):
                        after(pe, lo_done[b], i + 1)
                        for fill in range(FILLS):
                            after(pe, evacuated[b], i * FILLS + max(fill - 3, 0))
                            for u in range(2):
                                t = 2 * fill + u
                                for k in range(KT):
                                    last = mm3(nc, ps[b][fill % 4][:, u, :], h_hi[:, k, t * P:(t + 1) * P],
                                               h_lo[:, k, t * P:(t + 1) * P], hi[b][:, k, :], lo[b][:, k, :], k == 0, k == KT - 1)
                            last.then_inc(product[b], 1)

            @block.scalar
            def _(act):
                with act.Fori(0, TURNS) as i:
                    for b in range(2):
                        for fill in range(FILLS):
                            o, first = fill // 2 % 2, 2 * fill % STORE
                            after(act, product[b], i * FILLS + fill + 1)
                            if first == 0:
                                after(act, stored[o], (i * 4 + 2 * b + fill // 4) * DMA)
                            nc.scalar.activation(out[o][:, first:first + 2, :], ps[b][fill % 4][:],
                                                 funcs[b]).then_inc(evacuated[b], 1)
                            if first:
                                after(act, evacuated[b], i * FILLS + fill + 1)
                                t = 2 * fill - first
                                act.dma_start(rows[b][:, t:t + STORE, bass.ds(i * W, W)], out[o][:]).then_inc(stored[o], DMA)
                for o in range(2):
                    after(act, stored[o], TURNS * 4 * DMA)


PIECES = {
    "query": (COL_Q, ACT.Silu, 1.0),
    "key_f": (COL_ZF, ACT.Sigmoid, -1.0),
    "key_b": (COL_ZB, ACT.Sigmoid, -1.0),
    "gate_f": (COL_GF, ACT.Silu, 1.0),
    "wave": (COL_U, ACT.Copy, 1.0),
}
OF_NEXT = ("query", "key_f", "key_b")
OF_THIS = ("gate_f", "wave")


def first_head(nc, w_in, h_hi, h_lo, scratch):
    with Room(nc, "first") as r:
        n = len(OF_NEXT)
        raw = [r.sb(f"raw{j}", [P, KT, P]) for j in range(n)]
        hi = [r.sb(f"hi{j}", [P, KT, P], F32R) for j in range(n)]
        lo = [r.sb(f"lo{j}", [P, KT, P], F32R) for j in range(n)]
        out = [r.sb(f"out{j}", [P, SEQ]) for j in range(2)]
        ps = [r.ps(f"ps{i}") for i in range(4)]
        w_here = [r.sem(f"w_here{j}") for j in range(n)]
        hi_done, lo_done, product, evacuated = (r.sem(s) for s in ("hi_done", "lo_done", "product", "evacuated"))
        stored = [r.sem(f"stored{j}") for j in range(n)]
        w_view = w_in[0].rearrange("(k p) n -> p k n", p=P)
        with nc.Block() as block:

            @block.sync
            def _(sp):
                for j, name in enumerate(OF_NEXT):
                    col = PIECES[name][0]
                    sp.dma_start(raw[j][:], w_view[:, :, col:col + P]).then_inc(w_here[j], DMA)

            @block.vector
            def _(v):
                for j in range(n):
                    v.wait_ge(w_here[j], DMA)
                    nc.vector.tensor_copy(hi[j][:], raw[j][:]).then_inc(hi_done, 1)
                    v.wait_ge(hi_done, j + 1)
                    nc.vector.tensor_tensor(lo[j][:], raw[j][:], hi[j][:].bitcast(F32), ALU.subtract).then_inc(lo_done, 1)

            @block.tensor
            def _(pe):
                for j in range(n):
                    pe.wait_ge(lo_done, j + 1)
                    for g in range(NG):
                        if j:
                            pe.wait_ge(evacuated, (j - 1) * NG + g + 1)
                        for k in range(KT):
                            last = mm3(nc, ps[g][:], hi[j][:, k, :], lo[j][:, k, :], h_hi[:, k, g * GRP:(g + 1) * GRP],
                                       h_lo[:, k, g * GRP:(g + 1) * GRP], k == 0, k == KT - 1)
                        last.then_inc(product, 1)

            @block.scalar
            def _(act):
                for j, name in enumerate(OF_NEXT):
                    if j >= 2:
                        act.wait_ge(stored[j - 2], DMA)
                    for g in range(NG):
                        act.wait_ge(product, j * NG + g + 1)
                        nc.scalar.activation(out[j % 2][:, g * GRP:(g + 1) * GRP], ps[g][:], PIECES[name][1],
                                             scale=PIECES[name][2]).then_inc(evacuated, 1)
                    act.wait_ge(evacuated, (j + 1) * NG)
                    act.dma_start(scratch[name][0:P, :], out[j % 2][:]).then_inc(stored[j], DMA)
                for j in range(n):
                    act.wait_ge(stored[j], DMA)


LEVELS = (1, 2, 4, 8, 16, 32, 64)
MASKED = 6


def score_masks():
    s, t = np.arange(P)[:, None], np.arange(P)[None, :]
    masks = np.zeros((P, 2, MASKED, P), np.float32)
    for d in range(2):
        a, b = (s, t) if d == 0 else (P - 1 - s, P - 1 - t)
        masks[:, d, 0] = a == b
        for i, n in enumerate(LEVELS[:MASKED - 2]):
            masks[:, d, i + 1] = (b // n % 2 == 1) & (a // n == b // n - 1)
        masks[:, d, MASKED - 1] = a // 16 < b // 16
    return masks


def heads(nc, w_in, one_minus_lb, ident, masks, h_hi, h_lo, states, value_rows, scratch, o_rows):
    PROD, OPS, CHAIN, TOT = 11, 9, 5, 7
    KEYS_T, INC, OUT = 9, 10, 11
    PIECE_SLOT = (0, 1, 0, 1, 0)
    HALVES = 2 * NG * len(PIECE_SLOT)
    PER_STEP = HALVES // NG
    with Room(nc, "head") as r:
        raw = r.sb("raw", [P, KT, P])
        hi = [r.sb(f"hi{b}", [P, KT, P], F32R) for b in range(2)]
        lo = [r.sb(f"lo{b}", [P, KT, P], F32R) for b in range(2)]
        projected = [r.sb(f"projected{b}", [P, GRP]) for b in range(2)]
        query = [[r.sb(f"query{d}{b}", [P, GRP]) for b in range(2)] for d in range(2)]
        key = [[r.sb(f"key{d}{b}", [P, GRP]) for b in range(2)] for d in range(2)]
        value = [[r.sb(f"value{d}{b}", [P, TPG, P]) for b in range(2)] for d in range(2)]
        gate = [r.sb(f"gate{d}", [P, GRP]) for d in range(2)]
        total = [r.sb(f"total{d}", [P, GRP]) for d in range(2)]
        score = [r.sb(f"score{d}", [P, TPG, P]) for d in range(2)]
        key_t = [r.sb(f"key_t{d}", [P, TPG, P]) for d in range(2)]
        state = [r.sb(f"state{d}", [P, TPG + 1, P]) for d in range(2)]
        o = [r.sb(f"o{d}", [P, TPG, P]) for d in range(2)]
        ps_proj = [r.ps(f"ps_proj{b}") for b in range(2)]
        ps = [[r.ps(f"ps{d}{i}", [P, TPG, P]) for i in range(3)] for d in range(2)]
        w_here = r.sem("w_here", from_zero=True)
        hi_done, lo_done = r.sem("hi_done"), r.sem("lo_done")
        proj_done, proj_copied = r.sem("proj_done"), r.sem("proj_copied")
        proj_stored = [r.sem(f"proj_stored{b}") for b in range(2)]
        loaded = [[r.sem(f"loaded{d}{b}") for b in range(2)] for d in range(2)]
        cleared = r.sem("cleared")
        product = [r.sem(f"product{d}") for d in range(2)]
        operand = [r.sem(f"operand{d}") for d in range(2)]
        gated = [r.sem(f"gated{d}") for d in range(2)]
        totalled = [r.sem(f"totalled{d}") for d in range(2)]
        copied = [r.sem(f"copied{d}") for d in range(2)]
        chained = [r.sem(f"chained{d}") for d in range(2)]
        start_here = [r.sem(f"start_here{d}") for d in range(2)]
        key_t_copied = [r.sem(f"key_t_copied{d}") for d in range(2)]
        o_copied = [r.sem(f"o_copied{d}") for d in range(2)]
        o_stored = [r.sem(f"o_stored{d}") for d in range(2)]
        w_view = w_in[0].rearrange("(k p) n -> p k n", p=P)
        key_names = ("key_f", "key_b")
        LOADS = 3

        def group_of(d, g):
            return g if d == 0 else NG - 1 - g

        def in_time(ap, d):
            return ap if d == 0 else ap[:, ::-1]

        def total_of(d, b):
            if b == 1:
                return in_time(gate[d][:], d)
            at = GRP - 2 * GRP // b
            return total[d][:, at:at + GRP // b]

        def pieces(h, last):
            return ([] if last else [(name, h + 1) for name in OF_NEXT]) + [(name, h) for name in OF_THIS]

        def halves_at(g, slot, last):
            n = g * PER_STEP + slot
            return n if n < 2 * NG * len(pieces(0, last)) else None

        def slot_of(j, last):
            return PIECE_SLOT[j + (len(OF_NEXT) if last else 0)]

        r.start_at_one()
        with nc.Block() as block:

            @block.gpsimd
            def _(pool):
                for d in range(2):
                    pool.memset(score[d][:], 0.0).then_inc(cleared, 1)

                def turn(h, last):
                    for j, (name, head) in enumerate(pieces(h, last)):
                        after(pool, lo_done, 5 * h + j)
                        pool.dma_start(raw[:], w_view[:, :, bass.ds(PIECES[name][0] + head * P, P)]).then_inc(w_here, DMA)

                with pool.Fori(0, HEADS - 1) as h:
                    turn(h, False)
                turn(HEADS - 1, True)

            @block.sync
            def _(sp):
                def start_state(h):
                    for d in range(2):
                        after(sp, chained[d], CHAIN * NG * h)
                        sp.dma_start(state[d][:, TPG, :], states[d][bass.ds(h * P, P), :]).then_inc(start_here[d], DMA)

                def load(h, g):
                    for d in range(2):
                        t = group_of(d, g) * GRP
                        sem, b = loaded[d][g % 2], g % 2
                        sp.dma_start(query[d][b][:], scratch["query"][bass.ds(h * P, P), t:t + GRP]).then_inc(sem, DMA)
                        sp.dma_start(key[d][b][:], scratch[key_names[d]][bass.ds(h * P, P), t:t + GRP]).then_inc(sem, DMA)
                        sp.dma_start(value[d][b][:], value_rows[t:t + GRP, bass.ds(h * P, P)].rearrange("(t p) n -> p t n", p=P)
                                     ).then_inc(sem, DMA)

                def turn(h, last):
                    start_state(h)
                    for g in range(NG):
                        if g == NG - 1 and last:
                            break
                        for d in range(2):
                            after(sp, product[d], PROD * (NG * h + g))
                        if g < NG - 1:
                            load(h, g + 1)
                        else:
                            for b in range(2):
                                after(sp, proj_stored[b], (10 * h + 6) * DMA)
                            load(h + 1, 0)

                load(0, 0)
                with sp.Fori(0, HEADS - 1) as h:
                    turn(h, False)
                turn(HEADS - 1, True)

            @block.tensor
            def _(pe):
                def project_half(h, last, g, slot):
                    n = halves_at(g, slot, last)
                    if n is None:
                        return
                    unit, half = n // 2, n % 2
                    j, group = unit // NG, unit % NG
                    b = slot_of(j, last)
                    if group == 0 and half == 0:
                        after(pe, lo_done, 5 * h + j + 1)
                    if half == 0:
                        if unit < 2:
                            after(pe, proj_copied, 20 * h)
                        else:
                            after(pe, proj_copied, 20 * h + unit - 1)
                    for k in range(half * KT // 2, (half + 1) * KT // 2):
                        done = mm3(nc, ps_proj[unit % 2][:], hi[b][:, k, :], lo[b][:, k, :],
                                   h_hi[:, k, group * GRP:(group + 1) * GRP], h_lo[:, k, group * GRP:(group + 1) * GRP],
                                   k == 0, k == KT - 1)
                    if half == 1:
                        done.then_inc(proj_done, 1)

                def tile(ap, t):
                    return ap[:, t * P:(t + 1) * P]

                def step(h, g, last):
                    n, b = NG * h + g, g % 2
                    for d in range(2):
                        after(pe, loaded[d][b], (2 * h + g // 2 + 1) * LOADS * DMA)
                        after(pe, operand[d], OPS * n + 1)
                        for t in range(TPG):
                            done = nc.tensor.matmul(ps[d][0][:, t, :], tile(key[d][b], t), tile(query[d][b], t), start=True, stop=True)
                        done.then_inc(product[d], 1)
                    project_half(h, last, g, 0)
                    for i in range(5):
                        for d in range(2):
                            after(pe, operand[d], OPS * n + 2 + i)
                            if i == 0:
                                after(pe, chained[d], CHAIN * n)
                            elif i == 1:
                                after(pe, o_copied[d], n)
                            else:
                                after(pe, copied[d], MASKED * n + i - 1)
                            for t in range(TPG):
                                done = nc.tensor.matmul(ps[d][(i + 1) % 3][:, t, :], tile(key[d][b], t), tile(query[d][b], t),
                                                        start=True, stop=True)
                            done.then_inc(product[d], 1)
                        project_half(h, last, g, 1 + i)
                    for i, size in ((5, 32), (6, 64)):
                        for d in range(2):
                            after(pe, operand[d], OPS * n + 2 + i)
                            for t in range(TPG):
                                for pair in range(P // (2 * size)):
                                    s, q = (2 * pair, 2 * pair + 1) if d == 0 else (2 * pair + 1, 2 * pair)
                                    s, q = slice(s * size, (s + 1) * size), slice(q * size, (q + 1) * size)
                                    done = nc.tensor.matmul(ps[d][2][s, t, q], tile(key[d][b], t)[:, s], tile(query[d][b], t)[:, q],
                                                            start=True, stop=True)
                            done.then_inc(product[d], 1)
                        project_half(h, last, g, 1 + i)
                    for d in range(2):
                        after(pe, operand[d], OPS * n + OPS)
                        after(pe, copied[d], MASKED * n + 4)
                        for t in range(TPG):
                            done = nc.tensor.transpose(ps[d][0][:, t, :], tile(key[d][b], t), ident[:])
                        done.then_inc(product[d], 1)
                    project_half(h, last, g, 8)
                    for d in range(2):
                        after(pe, key_t_copied[d], n + 1)
                        after(pe, copied[d], MASKED * n + 5)
                        for t in range(TPG):
                            done = nc.tensor.matmul(ps[d][1][:, t, :], key_t[d][:, t, :], value[d][b][:, t, :], start=True, stop=True)
                        done.then_inc(product[d], 1)
                    project_half(h, last, g, 9)
                    for d in range(2):
                        after(pe, copied[d], MASKED * n + MASKED)
                        after(pe, chained[d], CHAIN * n + TPG)
                        for t in range(TPG):
                            before = t if d == 0 else TPG - 1 - t
                            nc.tensor.matmul(ps[d][2][:, t, :], score[d][:, t, :], value[d][b][:, t, :], start=True, stop=False)
                            done = nc.tensor.matmul(ps[d][2][:, t, :], tile(query[d][b], t), state[d][:, before, :], start=False, stop=True)
                        done.then_inc(product[d], 1)

                with pe.Fori(0, HEADS - 1) as h:
                    for g in range(NG):
                        step(h, g, False)
                for g in range(NG):
                    step(HEADS - 1, g, True)

            @block.scalar
            def _(act):
                def split_high(h, j, last):
                    act.wait_ge(w_here, (5 * h + j + 1) * DMA)
                    free = freed_units(h, j, last)
                    after(act, proj_done, free)
                    nc.scalar.activation(hi[slot_of(j, last)][:], raw[:], ACT.Copy).then_inc(hi_done, 1)

                def freed_units(h, j, last):
                    if j == 0:
                        return 20 * h
                    return 20 * h + NG * (j - 1) if not last or j > 1 else 20 * h

                def evacuate(h, last, g, slot):
                    n = halves_at(g, slot, last)
                    if n is None or n % 2 == 0:
                        return
                    unit = n // 2
                    j, group = unit // NG, unit % NG
                    name, head = pieces(h, last)[j]
                    after(act, proj_done, 20 * h + unit + 1)
                    after(act, proj_stored[unit % 2], (10 * h + unit // 2) * DMA)
                    nc.scalar.activation(projected[unit % 2][:], ps_proj[unit % 2][:], PIECES[name][1],
                                         scale=PIECES[name][2]).then_inc(proj_copied, 1)
                    after(act, proj_copied, 20 * h + unit + 1)
                    act.dma_start(scratch[name][bass.ds(head * P, P), group * GRP:(group + 1) * GRP],
                                  projected[unit % 2][:]).then_inc(proj_stored[unit % 2], DMA)
                    if group == 0 and j + 1 < len(pieces(h, last)):
                        split_high(h, j + 1, last)

                def step(h, g, last):
                    n = NG * h + g
                    for slot in range(9):
                        evacuate(h, last, g, slot)
                    for d in range(2):
                        after(act, product[d], PROD * n + KEYS_T)
                        nc.scalar.activation(key_t[d][:], ps[d][0][:], ACT.Copy).then_inc(key_t_copied[d], 1)
                    evacuate(h, last, g, 9)
                    for d in range(2):
                        after(act, product[d], PROD * n + OUT)
                        after(act, o_stored[d], n * DMA)
                        nc.scalar.activation(o[d][:], ps[d][2][:], ACT.Copy).then_inc(o_copied[d], 1)
                    for d in range(2):
                        after(act, o_copied[d], n + 1)
                        t = group_of(d, g) * GRP
                        act.dma_start(o_rows[d][t:t + GRP, bass.ds(h * P, P)].rearrange("(t p) n -> p t n", p=P),
                                      o[d][:]).then_inc(o_stored[d], DMA)

                def turn(h, last):
                    split_high(h, 0, last)
                    for g in range(NG):
                        step(h, g, last)

                with act.Fori(0, HEADS - 1) as h:
                    turn(h, False)
                turn(HEADS - 1, True)
                for b in range(2):
                    after(act, proj_stored[b], (10 * (HEADS - 1) + NG * len(OF_THIS) // 2) * DMA)
                for d in range(2):
                    after(act, o_stored[d], NG * HEADS * DMA)

            @block.vector
            def _(v):
                def split_low(h, j, last):
                    after(v, hi_done, 5 * h + j + 1)
                    b = slot_of(j, last)
                    nc.vector.tensor_tensor(lo[b][:], raw[:], hi[b][:].bitcast(F32), ALU.subtract).then_inc(lo_done, 1)

                def split_due(g, level, last):
                    for j in range(0, len(pieces(0, last)) - 1):
                        half = 2 * NG * j + 2
                        if (half // PER_STEP, max(1, min(half % PER_STEP, 7))) == (g, level):
                            return j + 1
                    return None

                def copy_scores(d, c, bank):
                    nc.vector.copy_predicated(score[d][:], masks[:, d, c:c + 1, :].to_broadcast([P, TPG, P]), ps[d][bank][:]
                                              ).then_inc(copied[d], 1)

                def step(h, g, last):
                    n, b = NG * h + g, g % 2
                    for d in range(2):
                        after(v, loaded[d][b], (2 * h + g // 2 + 1) * LOADS * DMA)
                        nc.vector.tensor_scalar(key[d][b][:], key[d][b][:], one_minus_lb[:, d, bass.ds(h, 1)], None,
                                                ALU.mult).then_inc(operand[d], 1)
                    for d in range(2):
                        after(v, operand[d], OPS * n + 1)
                        nc.vector.tensor_scalar(gate[d][:], key[d][b][:], -1.0, 1.0, ALU.mult, ALU.add).then_inc(gated[d], 1)
                    for d in range(2):
                        after(v, gated[d], 2 * n + 1)
                        nc.vector.tensor_scalar(gate[d][:], gate[d][:], F_MIN, None, ALU.max).then_inc(gated[d], 1)
                    for d in range(2):
                        after(v, gated[d], 2 * n + 2)
                        after(v, product[d], PROD * n + 1)
                        nc.vector.tensor_tensor(query[d][b][:], query[d][b][:], gate[d][:], ALU.mult).then_inc(operand[d], 1)
                    for d in range(2):
                        copy_scores(d, 0, 0)
                    for i, size in enumerate(LEVELS):
                        for d in range(2):
                            blocks = "p (n two b) -> p n two b"
                            qs = in_time(query[d][b][:], d).rearrange(blocks, two=2, b=size)
                            ks = in_time(key[d][b][:], d).rearrange(blocks, two=2, b=size)
                            tot = total_of(d, size).rearrange("p (n two o) -> p n two o", two=2, o=1)
                            shape = [P, GRP // (2 * size), size]
                            after(v, product[d], PROD * n + 2 + i)
                            after(v, operand[d], OPS * n + 2 + i)
                            if i:
                                after(v, totalled[d], TOT * n + i)
                            nc.vector.tensor_tensor(qs[:, :, 1, :], qs[:, :, 1, :], tot[:, :, 0, :].to_broadcast(shape), ALU.mult)
                            nc.vector.tensor_tensor(ks[:, :, 0, :], ks[:, :, 0, :], tot[:, :, 1, :].to_broadcast(shape),
                                                    ALU.mult).then_inc(operand[d], 1)
                            after(v, copied[d], MASKED * n + min(i + 1, MASKED - 1))
                            nc.vector.tensor_tensor(total_of(d, 2 * size), tot[:, :, 0, 0], tot[:, :, 1, 0],
                                                    ALU.mult).then_inc(totalled[d], 1)
                        if i < MASKED - 2:
                            for d in range(2):
                                copy_scores(d, i + 1, (i + 1) % 3)
                        due = split_due(g, i + 1, last)
                        if due is not None:
                            split_low(h, due, last)
                    for d in range(2):
                        copy_scores(d, MASKED - 1, 2)
                    for d in range(2):
                        after(v, chained[d], CHAIN * n)
                        if g == 0:
                            after(v, start_here[d], (h + 1) * DMA)
                        after(v, product[d], PROD * n + 1)
                        nc.vector.tensor_copy(state[d][:, 0, :], state[d][:, TPG, :]).then_inc(chained[d], 1)
                    for j in range(TPG):
                        for d in range(2):
                            t = j if d == 0 else TPG - 1 - j
                            after(v, chained[d], CHAIN * n + j + 1)
                            if j == 0:
                                after(v, product[d], PROD * n + INC)
                                after(v, totalled[d], TOT * n + TOT)
                            nc.vector.scalar_tensor_tensor(state[d][:, j + 1, :], state[d][:, j, :], total_of(d, P)[:, j:j + 1],
                                                           ps[d][1][:, t, :], ALU.mult, ALU.add).then_inc(chained[d], 1)

                def turn(h, last):
                    split_low(h, 0, last)
                    for g in range(NG):
                        step(h, g, last)

                v.wait_ge(cleared, 3)
                with v.Fori(0, HEADS - 1) as h:
                    turn(h, False)
                turn(HEADS - 1, True)


HALF, QUART = SEQ // 2, SEQ // 4
QT = QUART // P


def wave_tables():
    t, m = np.arange(QUART, dtype=np.int64)[:, None], np.arange(QUART, dtype=np.int64)[None, :]
    turn = lambda k: 2 * np.pi * (t * k % SEQ) / SEQ
    tab = np.stack([np.cos(turn(2 * m)), np.cos(turn(2 * m + 1)), np.sin(turn(2 * m)), np.sin(turn(2 * m + 1))])
    tab[3, 0] = (-1.0) ** m[0]
    c = np.arange(FC, dtype=np.int64)
    ang = 2 * np.pi * (c[:, None] * c[None, :] % FC) / FC
    chan = np.stack([np.cos(ang), np.sin(ang)]) / np.sqrt(SEQ * FC)
    sign = (-1.0) ** np.arange(QUART)
    return (tab.reshape(4, QT, P, QUART).transpose(2, 0, 1, 3).astype(np.float32),
            chan.reshape(2, 2, P, FC).transpose(2, 0, 1, 3).astype(np.float32),
            np.broadcast_to(sign.reshape(QT, P).T[:, :, None], (P, QT, 2)).astype(np.float32),
            sign[None, :].astype(np.float32))


def fourier(nc, tables_in, chan_in, sign_cols_in, sign_row_in, w_fourier, b_cols_in, wave, gate_f, y_f):
    CC = FC // P
    with Room(nc, "four") as r:
        tab_hi = [r.sb(f"tab_hi{a}", [P, QT, QUART], F32R) for a in range(4)]
        tab_lo = [r.sb(f"tab_lo{a}", [P, QT, QUART], F32R) for a in range(4)]
        sign_cols = r.sb("sign_cols", [P, QT, 2], F32R)
        sign_row = r.sb("sign_row", [1, QUART])
        b_cols = r.sb("b_cols", [P, FW // P])
        chan = r.sb("chan", [P, 2, CC, FC])
        with Room(nc, "tab") as s:
            raw = [s.sb(f"raw{a}", [P, QT, QUART]) for a in range(4)]
            raw_sign = s.sb("raw_sign", [P, QT, 2])
            here, small_here = [s.sem(f"here{a}") for a in range(4)], s.sem("small_here")
            hi_done, lo_done = s.sem("hi_done"), s.sem("lo_done")
            with nc.Block() as block:

                @block.sync
                def _(sp):
                    for a in range(4):
                        sp.dma_start(raw[a][:], tables_in[:, a]).then_inc(here[a], DMA)
                    for dst, src in ((raw_sign, sign_cols_in), (sign_row, sign_row_in), (b_cols, b_cols_in), (chan, chan_in)):
                        sp.dma_start(dst[:], src).then_inc(small_here, DMA)
                    sp.wait_ge(small_here, 4 * DMA)

                @block.scalar
                def _(act):
                    for a in range(4):
                        act.wait_ge(here[a], DMA)
                        nc.scalar.activation(tab_hi[a][:], raw[a][:], ACT.Copy).then_inc(hi_done, 1)
                    act.wait_ge(small_here, 4 * DMA)
                    nc.scalar.activation(sign_cols[:], raw_sign[:], ACT.Copy).then_inc(hi_done, 1)

                @block.vector
                def _(v):
                    for a in range(4):
                        v.wait_ge(hi_done, a + 1)
                        nc.vector.tensor_tensor(tab_lo[a][:], raw[a][:], tab_hi[a][:].bitcast(F32), ALU.subtract).then_inc(lo_done, 1)

        u = r.sb("u", [P, CC, SEQ])
        once = [r.sb(f"once{i}", [P, CC, HALF + 1]) for i in range(2)]
        fold_hi, fold_lo = r.sb("fold_hi", [P, CC, SEQ], F32R), r.sb("fold_lo", [P, CC, SEQ], F32R)
        w = r.sb("w", [P, CC, FC])
        cw = r.sb("cw", [P, CC, FC])
        cw_hi, cw_lo = r.sb("cw_hi", [P, 2, CC, FC], F32R), r.sb("cw_lo", [P, 2, CC, FC], F32R)
        mid = r.sb("mid", [1, FC])
        p_hi = [r.sb(f"p_hi{a}", [P, QT, FC], F32R) for a in range(4)]
        p_lo = [r.sb(f"p_lo{a}", [P, QT, FC], F32R) for a in range(4)]
        sine = r.sb("sine", [P, 2, QUART])
        y = r.sb("y", [P, SEQ])
        g = [r.sb(f"g{c}", [P, SEQ]) for c in range(CC)]
        ps_y = [r.ps(f"ps_y{a}") for a in range(4)]
        ps_p = [r.ps(f"ps_p{i}", [P, 2, FC]) for i in range(2)]
        ps_w = [r.ps(f"ps_w{i}", [P, CC, FC]) for i in range(2)]
        u_here, w_here = r.sem("u_here"), r.sem("w_here")
        g_here, stored = [r.sem(f"g_here{c}") for c in range(CC)], [r.sem(f"stored{c}") for c in range(CC)]
        once_done, fold_done, fold_hi_done, fold_lo_done = (r.sem(n) for n in ("once_done", "fold_done", "fold_hi_done", "fold_lo_done"))
        w_done, w_hi_done, w_lo_done, mid_done, mid_copied = (r.sem(n) for n in ("w_done", "w_hi_done", "w_lo_done", "mid_done", "mid_copied"))
        p_done, p_hi_done, p_lo_done = (r.sem(n) for n in ("p_done", "p_hi_done", "p_lo_done"))
        y_done, sine_copied, combined, top_done, top_copied, gated = (r.sem(n) for n in
                                                                     ("y_done", "sine_copied", "combined", "top_done", "top_copied", "gated"))
        set_once = r.sem("set_once")

        def array(ap, a):
            return ap[:, :, a * QUART:(a + 1) * QUART]

        r.start_at_one()
        with nc.Block() as block:

            @block.sync
            def _(sp):
                def load_u(at):
                    sp.dma_start(u[:], wave[bass.ds(at, FC), :].rearrange("(c p) t -> p c t", p=P)).then_inc(u_here, DMA)

                def load_w(at):
                    sp.dma_start(w[:], w_fourier[bass.ds(at, FC), :].rearrange("(c p) d -> p c d", p=P)).then_inc(w_here, DMA)

                def load_g(at, c):
                    sp.dma_start(g[c][:], gate_f[bass.ds(at, P), :]).then_inc(g_here[c], DMA)

                def turn(n, last):
                    at = [n * FC + c * P for c in range(CC)] if last else [sp.snap(n * FC + c * P) for c in range(CC)]
                    ahead = None if last else [sp.snap(n * FC + FC + c * P) for c in range(CC)]
                    if not last:
                        after(sp, fold_lo_done, n + 1)
                        load_u(ahead[0])
                        after(sp, w_done, 2 * n + 2)
                        load_w(ahead[0])
                    for c in range(CC):
                        after(sp, gated, 2 * n + c + 1)
                        sp.dma_start(y_f[bass.ds(at[c], P), :], g[c][:]).then_inc(stored[c], DMA)
                        if not last:
                            after(sp, stored[c], (n + 1) * DMA)
                            load_g(ahead[c], c)

                load_u(0)
                load_w(0)
                for c in range(CC):
                    load_g(c * P, c)
                with sp.Fori(0, FG - 1) as n:
                    turn(n, False)
                turn(FG - 1, True)
                for c in range(CC):
                    after(sp, stored[c], FG * DMA)

            @block.vector
            def _(v):
                def fold(n):
                    after(v, u_here, (n + 1) * DMA)
                    nc.vector.tensor_tensor(once[0][:, :, 1:HALF], u[:, :, 1:HALF], u[:, :, SEQ - 1:HALF:-1], ALU.add)
                    nc.vector.tensor_tensor(once[1][:, :, 1:HALF], u[:, :, 1:HALF], u[:, :, SEQ - 1:HALF:-1], ALU.subtract)
                    nc.vector.tensor_copy(once[0][:, :, 0:HALF + 1:HALF], u[:, :, 0:HALF + 1:HALF]).then_inc(once_done, 1)
                    after(v, once_done, n + 1)
                    for a, op in enumerate((ALU.add, ALU.subtract, ALU.subtract, ALU.add)):
                        src = once[a // 2]
                        nc.vector.tensor_tensor(array(u, a), src[:, :, 0:QUART], src[:, :, HALF:QUART:-1], op).then_inc(fold_done, 1)
                    after(v, fold_done, 5 * n + 4)
                    nc.vector.tensor_copy(u[:, :, 3 * QUART:3 * QUART + 1], once[1][:, :, QUART:QUART + 1]).then_inc(fold_done, 1)
                    after(v, fold_hi_done, n + 1)
                    nc.vector.tensor_tensor(fold_lo[:], u[:], fold_hi[:].bitcast(F32), ALU.subtract).then_inc(fold_lo_done, 1)

                def turn(n, last):
                    for i in range(2):
                        after(v, w_hi_done, 2 * n + i + 1)
                        nc.vector.tensor_tensor(cw_lo[:, i], ps_w[i][:], cw_hi[:, i].bitcast(F32), ALU.subtract).then_inc(w_lo_done, 1)
                    for f in range(8):
                        a, t = f // 2, f % 2 * 2
                        after(v, p_hi_done, 8 * n + f + 1)
                        nc.vector.tensor_tensor(p_lo[a][:, t:t + 2, :], ps_p[f % 2][:], p_hi[a][:, t:t + 2, :].bitcast(F32),
                                                ALU.subtract).then_inc(p_lo_done, 1)
                    if not last:
                        fold(n + 1)
                    for c in range(CC):
                        m = 2 * n + c
                        for odd in range(2):
                            after(v, sine_copied, 2 * m + odd + 1)
                            after(v, y_done, 4 * m + 2 * odd + 1)
                            after(v, gated, m)
                            cos, sin = ps_y[odd], sine[:, odd, :]
                            nc.vector.tensor_tensor(y[:, odd:HALF:2], cos[:], sin, ALU.subtract)
                            if odd:
                                out, cut = y[:, SEQ - 1:HALF:-2], 0
                            else:
                                out, cut = y[:, SEQ - 2:HALF:-2], 1
                            nc.vector.tensor_tensor(out, cos[:, cut:], sin[:, cut:], ALU.add).then_inc(combined, 1)
                        after(v, combined, 2 * m + 2)
                        after(v, top_copied, m + 1)
                        after(v, g_here[c], (n + 1) * DMA)
                        nc.vector.scalar_tensor_tensor(g[c][:], y[:], b_cols[:, bass.ds(2 * n + c, 1)], g[c][:],
                                                       ALU.add, ALU.mult).then_inc(gated, 1)

                nc.vector.memset(once[1][:, :, 0:1], 0.0)
                nc.vector.memset(once[1][:, :, HALF:HALF + 1], 0.0).then_inc(set_once, 1)
                v.wait_ge(set_once, 2)
                fold(0)
                with v.Fori(0, FG - 1) as n:
                    turn(n, False)
                turn(FG - 1, True)

            @block.scalar
            def _(act):
                def split_fold(n):
                    after(act, fold_done, 5 * n + 5)
                    after(act, p_done, 8 * n)
                    nc.scalar.activation(fold_hi[:], u[:], ACT.Copy).then_inc(fold_hi_done, 1)

                def turn(n, last):
                    for i in range(2):
                        after(act, w_done, 2 * n + i + 1)
                        after(act, p_done, 8 * n)
                        if i == 0:
                            nc.scalar.activation(cw[:], ps_w[0][:], ACT.Copy).then_inc(mid_copied, 1)
                        nc.scalar.activation(cw_hi[:, i], ps_w[i][:], ACT.Copy).then_inc(w_hi_done, 1)
                    after(act, mid_done, n + 1)
                    after(act, y_done, 8 * n)
                    nc.scalar.activation(mid[0:1, :], ps_w[0][0:1, 0, :], ACT.Copy).then_inc(mid_copied, 1)
                    for f in range(8):
                        a, t = f // 2, f % 2 * 2
                        after(act, p_done, 8 * n + f + 1)
                        after(act, top_done, 2 * n)
                        nc.scalar.activation(p_hi[a][:, t:t + 2, :], ps_p[f % 2][:], ACT.Copy).then_inc(p_hi_done, 1)
                    if not last:
                        split_fold(n + 1)
                    for c in range(CC):
                        m = 2 * n + c
                        for odd in range(2):
                            after(act, y_done, 4 * m + 2 * odd + 2)
                            after(act, combined, 2 * m)
                            nc.scalar.activation(sine[:, odd, :], ps_y[2 + odd][:], ACT.Copy).then_inc(sine_copied, 1)
                        after(act, top_done, m + 1)
                        after(act, gated, m)
                        nc.scalar.activation(y[:, HALF:HALF + 1], ps_w[1][:, 0, 0:1], ACT.Copy).then_inc(top_copied, 1)

                split_fold(0)
                with act.Fori(0, FG - 1) as n:
                    turn(n, False)
                turn(FG - 1, True)

            @block.tensor
            def _(pe):
                with pe.Fori(0, FG) as n:
                    after(pe, w_here, (n + 1) * DMA)
                    after(pe, top_copied, 2 * n)
                    for i in range(2):
                        for m in range(CC):
                            for k in range(CC):
                                done = nc.tensor.matmul(ps_w[i][:, m, :], chan[:, i, k, m * P:(m + 1) * P], w[:, k, :],
                                                        start=k == 0, stop=k == CC - 1)
                        done.then_inc(w_done, 1)
                    after(pe, mid_copied, 2 * n + 1)
                    after(pe, w_lo_done, 2 * n + 2)
                    after(pe, fold_lo_done, n + 1)
                    for k in range(CC):
                        done = nc.tensor.matmul(ps_w[0][0:1, 0, :], once[0][:, k, QUART:QUART + 1], cw[:, k, :],
                                                start=k == 0, stop=k == CC - 1)
                    done.then_inc(mid_done, 1)
                    for f in range(8):
                        a = f // 2
                        after(pe, p_lo_done, 8 * n + max(f - 1, 0))
                        for t in range(2):
                            for k in range(CC):
                                at = slice(a * QUART + (f % 2 * 2 + t) * P, a * QUART + (f % 2 * 2 + t + 1) * P)
                                done = mm3(nc, ps_p[f % 2][:, t, :], fold_hi[:, k, at], fold_lo[:, k, at],
                                           cw_hi[:, a // 2, k, :], cw_lo[:, a // 2, k, :], k == 0, k == CC - 1)
                        done.then_inc(p_done, 1)
                    for c in range(CC):
                        m = 2 * n + c
                        ch = slice(c * P, (c + 1) * P)
                        after(pe, combined, 2 * m)
                        after(pe, sine_copied, 2 * m)
                        after(pe, p_lo_done, 8 * n + 8)
                        after(pe, mid_copied, 2 * n + 2)
                        for a in (0, 2, 1, 3):
                            for t in range(QT):
                                done = mm3(nc, ps_y[a][:], p_hi[a][:, t, ch], p_lo[a][:, t, ch], tab_hi[a][:, t, :], tab_lo[a][:, t, :],
                                           t == 0, t == QT - 1 and a != 0)
                            if a == 0:
                                done = nc.tensor.matmul(ps_y[0][:], mid[0:1, ch], sign_row[0:1, :], start=False, stop=True)
                            done.then_inc(y_done, 1)
                        after(pe, top_copied, m)
                        for t in range(QT):
                            nc.tensor.matmul(ps_w[1][:, 0, 0:2], p_hi[0][:, t, ch], sign_cols[:, t, :], start=t == 0, stop=False)
                            nc.tensor.matmul(ps_w[1][:, 0, 0:2], p_lo[0][:, t, ch], sign_cols[:, t, :], start=False, stop=False)
                        nc.tensor.matmul(ps_w[1][:, 0, 0:2], mid[0:1, ch], sign_row[0:1, 0:3:2], start=False, stop=True
                                         ).then_inc(top_done, 1)


def output(nc, ident, x_rows, row_code, col_code, w_out, o_rows, gate_rows_a, y_f, gate_rows, hgrn_cols_in, final_norm_w, out_rows):
    KO = MIX // P
    H = D // 2
    with Room(nc, "out") as r:
        w_hi = r.sb("w_hi", [P, KO, D], F32R)
        w_lo = r.sb("w_lo", [P, KO, D], F32R)
        hn = r.sb("hn", [P, HEADS])
        eps = r.sb("eps", [P, 1])
        res_gate = r.sb("res_gate", [P, D])
        fnw = r.sb("fnw", [P, D])
        col = r.sb("col", [P, H])
        with Room(nc, "wout") as s:
            RING = 8
            raw = [s.sb(f"raw{i}", [P, D]) for i in range(RING)]
            here = [s.sem(f"here{i}") for i in range(RING)]
            hi_done, lo_done, small_here, eps_set = (s.sem(n) for n in ("hi_done", "lo_done", "small_here", "eps_set"))
            w_view = w_out[0].rearrange("(k p) n -> k p n", p=P)
            with nc.Block() as block:

                @block.sync
                def _(sp):
                    for k in range(KO):
                        if k >= RING:
                            sp.wait_ge(lo_done, k - RING + 1)
                        sp.dma_start(raw[k % RING][:], w_view[k]).then_inc(here[k % RING], DMA)

                @block.gpsimd
                def _(pool):
                    pool.memset(eps[:], EPS).then_inc(eps_set, 1)

                @block.scalar
                def _(act):
                    act.dma_start(hn[:], hgrn_cols_in).then_inc(small_here, DMA)
                    act.dma_start(res_gate[:], gate_rows).then_inc(small_here, DMA)
                    act.dma_start(fnw[:], row_on_all(final_norm_w, D)).then_inc(small_here, DMA)
                    for i in range(P // GRID_W):
                        act.dma_start(col[i * GRID_W:(i + 1) * GRID_W, :], col_code).then_inc(small_here, DMA)
                    for k in range(KO):
                        act.wait_ge(here[k % RING], (k // RING + 1) * DMA)
                        nc.scalar.activation(w_hi[:, k, :], raw[k % RING][:], ACT.Copy).then_inc(hi_done, 1)
                    act.wait_ge(small_here, 5 * DMA)

                @block.vector
                def _(v):
                    for k in range(KO):
                        v.wait_ge(hi_done, k + 1)
                        nc.vector.tensor_tensor(w_lo[:, k, :], raw[k % RING][:], w_hi[:, k, :].bitcast(F32),
                                                ALU.subtract).then_inc(lo_done, 1)

        o = [[r.sb(f"o{d}{b}", [P, D]) for b in range(2)] for d in range(2)]
        ga = [r.sb(f"ga{b}", [P, D]) for b in range(2)]
        x = [r.sb(f"x{b}", [P, D]) for b in range(2)]
        row = r.sb("row", [P, H])
        yf = r.sb("yf", [P, KT, P])
        work = r.sb("work", [P, D])
        y_hi, y_lo = [r.sb(f"y_hi{i}", [P, KT, P], F32R) for i in range(2)], [r.sb(f"y_lo{i}", [P, KT, P], F32R) for i in range(2)]
        tmp = r.sb("tmp", [P, D])
        stat = r.sb("stat", [P, 3, HEADS])
        fin = r.sb("fin", [P, 3])
        ps_t = [r.ps(f"ps_t{i}", [P, KT // 2, P]) for i in range(2)]
        ps_o = [[r.ps(f"ps_o{b}{i}") for i in range(2)] for b in range(2)]
        o_here, x_here, out_stored, products_used = ([r.sem(f"{n}{b}") for b in range(2)] for n in
                                                     ("o_here", "x_here", "out_stored", "products_used"))
        (yf_here, summed, coded, squared, reduced, rooted, inverted, scaled, gated, turned, staged, f_hi, f_lo, a_hi, a_lo,
         f_half, a_half, residual, row_squared, row_rooted, row_inverted, finished, tmp_done) = (r.sem(n) for n in (
             "yf_here", "summed", "coded", "squared", "reduced", "rooted", "inverted", "scaled", "gated", "turned", "staged",
             "f_hi", "f_lo", "a_hi", "a_lo", "f_half", "a_half", "residual", "row_squared", "row_rooted", "row_inverted",
             "finished", "tmp_done"))
        by_head = lambda ap: ap.rearrange("p (h n) -> p h n", h=HEADS)
        r.start_at_one()
        with nc.Block() as block:

            @block.sync
            def _(sp):
                with sp.Fori(0, NT // 2) as i:
                    for b in range(2):
                        t = 2 * i + b
                        tok = bass.ds(sp.snap(t * P), P)
                        codes = [bass.ds(sp.snap(t * 2 + half), 1) for half in range(2)]
                        after(sp, turned, 2 * i)
                        for d in range(2):
                            sp.dma_start(o[d][b][:], o_rows[d][tok, :]).then_inc(o_here[b], DMA)
                        sp.dma_start(ga[b][:], gate_rows_a[tok, :]).then_inc(o_here[b], DMA)
                        after(sp, out_stored[b], i * DMA)
                        sp.dma_start(x[b][:], x_rows[tok, :]).then_inc(x_here[b], DMA)
                        after(sp, coded, t)
                        for half in range(2):
                            sp.dma_start(row[half * GRID_W:(half + 1) * GRID_W, :],
                                         row_code[codes[half], :].to_broadcast([GRID_W, H])).then_inc(x_here[b], DMA)
                        sp.wait_ge(yf_here, 1)
                        after(sp, f_lo, t)
                        sp.dma_start(yf[:], y_f[:, tok].rearrange("(k p) t -> p k t", p=P)).then_inc(yf_here, DMA)

            @block.vector
            def _(v):
                def front(i, b):
                    t = 2 * i + b
                    oo = o[0][b]
                    after(v, o_here[b], (i + 1) * 3 * DMA)
                    nc.vector.tensor_tensor(oo[:], oo[:], o[1][b][:], ALU.add).then_inc(summed, 1)
                    after(v, x_here[b], (i + 1) * 3 * DMA)
                    nc.vector.tensor_tensor(x[b][:, 0:H], x[b][:, 0:H], row[:], ALU.add)
                    nc.vector.tensor_tensor(x[b][:, H:D], x[b][:, H:D], col[:], ALU.add).then_inc(coded, 1)
                    after(v, squared, t + 1)
                    nc.vector.tensor_reduce(stat[:, 0, :], by_head(work[:]), AX.X, ALU.add).then_inc(reduced, 1)
                    after(v, yf_here, (t + 1) * DMA)
                    after(v, f_half, t)
                    nc.vector.tensor_copy(y_hi[1][:], yf[:]).then_inc(f_hi, 1)
                    after(v, rooted, t + 1)
                    nc.vector.reciprocal(stat[:, 2, :], stat[:, 1, :]).then_inc(inverted, 1)
                    after(v, f_hi, t + 1)
                    nc.vector.tensor_tensor(y_lo[1][:], yf[:], y_hi[1][:].bitcast(F32), ALU.subtract).then_inc(f_lo, 1)
                    after(v, inverted, t + 1)
                    inv = stat[:, 2, :].rearrange("p (h o) -> p h o", o=1).to_broadcast([P, HEADS, P])
                    nc.vector.tensor_tensor(by_head(oo[:]), by_head(oo[:]), inv, ALU.mult).then_inc(scaled, 1)
                    after(v, scaled, t + 1)
                    nc.vector.tensor_tensor(oo[:], oo[:], ga[b][:], ALU.mult).then_inc(gated, 1)

                def split_heads(t):
                    after(v, staged, t + 1)
                    after(v, a_half, t)
                    nc.vector.tensor_copy(y_hi[0][:], work[:].rearrange("p (k n) -> p k n", k=KT)).then_inc(a_hi, 1)
                    after(v, a_hi, t + 1)
                    nc.vector.tensor_tensor(y_lo[0][:], work[:].rearrange("p (k n) -> p k n", k=KT), y_hi[0][:].bitcast(F32),
                                            ALU.subtract).then_inc(a_lo, 1)

                def finish(i, b):
                    t = 2 * i + b
                    after(v, a_half, t + 1)
                    after(v, row_squared, t)
                    for j in range(2):
                        cols = slice(j * H, (j + 1) * H)
                        last = nc.vector.tensor_tensor(tmp[:, cols], ps_o[b][j][:], res_gate[:, cols], ALU.mult)
                    last.then_inc(products_used[b], 1)
                    after(v, products_used[b], i + 1)
                    nc.vector.tensor_tensor(x[b][:], x[b][:], tmp[:], ALU.add).then_inc(residual, 1)
                    after(v, row_rooted, t + 1)
                    nc.vector.reciprocal(fin[:, 2:3], fin[:, 1:2]).then_inc(row_inverted, 1)
                    after(v, row_inverted, t + 1)
                    nc.vector.scalar_tensor_tensor(x[b][:], x[b][:], fin[:, 2:3], fnw[:], ALU.mult, ALU.mult).then_inc(finished, 1)

                def turn(i, last):
                    front(i, 1)
                    split_heads(2 * i + 1)
                    finish(i, 0)
                    if not last:
                        front(i + 1, 0)
                        split_heads(2 * i + 2)
                    finish(i, 1)

                front(0, 0)
                split_heads(0)
                with v.Fori(0, NT // 2 - 1) as i:
                    turn(i, False)
                turn(NT // 2 - 1, True)

            @block.scalar
            def _(act):
                def front(i, b):
                    t = 2 * i + b
                    after(act, summed, t + 1)
                    after(act, a_lo, t)
                    nc.scalar.activation(work[:], o[0][b][:], ACT.Square).then_inc(squared, 1)
                    after(act, reduced, t + 1)
                    nc.scalar.activation(stat[:, 1, :], stat[:, 0, :], ACT.Sqrt, scale=1.0 / P, bias=eps[:, 0:1]).then_inc(rooted, 1)

                def stage_heads(t):
                    after(act, turned, t + 1)
                    for k in range(KT):
                        last = nc.scalar.activation(work[:, k * P:(k + 1) * P], ps_t[k // 4][:, k % 4, :], ACT.Copy, scale=hn[:, k:k + 1])
                    last.then_inc(staged, 1)

                def finish(i, b):
                    t = 2 * i + b
                    after(act, residual, t + 1)
                    nc.scalar.activation(tmp[:], x[b][:], ACT.Square, accum_out=fin[:, 0:1]).then_inc(row_squared, 1)
                    after(act, row_squared, t + 1)
                    nc.scalar.activation(fin[:, 1:2], fin[:, 0:1], ACT.Sqrt, scale=1.0 / D, bias=eps[:, 0:1]).then_inc(row_rooted, 1)
                    after(act, finished, t + 1)
                    act.dma_start(out_rows[bass.ds(t * P, P), :], x[b][:]).then_inc(out_stored[b], DMA)

                def turn(i, last):
                    front(i, 1)
                    stage_heads(2 * i + 1)
                    finish(i, 0)
                    if not last:
                        front(i + 1, 0)
                        stage_heads(2 * i + 2)
                    finish(i, 1)

                front(0, 0)
                stage_heads(0)
                with act.Fori(0, NT // 2 - 1) as i:
                    turn(i, False)
                turn(NT // 2 - 1, True)
                for b in range(2):
                    after(act, out_stored[b], NT // 2 * DMA)

            @block.tensor
            def _(pe):
                def transpose_heads(t, b):
                    after(pe, gated, t + 1)
                    after(pe, staged, t)
                    for k in range(KT):
                        last = nc.tensor.transpose(ps_t[k // 4][:, k % 4, :], o[0][b][:, k * P:(k + 1) * P], ident[:])
                    last.then_inc(turned, 1)

                def project(i, b):
                    t = 2 * i + b
                    after(pe, products_used[b], i)
                    for part, split, signal in ((1, f_lo, f_half), (0, a_lo, a_half)):
                        after(pe, split, t + 1)
                        for k in range(KT):
                            for j in range(2):
                                ko, cols = part * KT + k, slice(j * H, (j + 1) * H)
                                last = mm3(nc, ps_o[b][j][:], y_hi[part][:, k, :], y_lo[part][:, k, :], w_hi[:, ko, cols], w_lo[:, ko, cols],
                                           part == 1 and k == 0, part == 0 and k == KT - 1)
                        last.then_inc(signal, 1)

                def turn(i, last):
                    project(i, 0)
                    transpose_heads(2 * i + 1, 1)
                    project(i, 1)
                    if not last:
                        transpose_heads(2 * i + 2, 0)

                transpose_heads(0, 0)
                with pe.Fori(0, NT // 2 - 1) as i:
                    turn(i, False)
                turn(NT // 2 - 1, True)


def program(nc, x, ctx, w_ada, b_ada, w_in, w_fourier, w_out, final_norm_w, conds, b_ada_cols, norm_w_cols, bounds_cols,
            hgrn_cols, b_fourier_cols, row_code, col_code, masks_in, tables, chan_tables, sign_cols, sign_row, out):
    def scratch(name, shape):
        return nc.dram_tensor(name, shape, F32).ap()

    gate_rows = scratch("residual_gate", (P, D))
    states = [scratch(f"context_state{d}", (HG, P)) for d in range(2)]
    value_rows, gate_rows_a = scratch("value_rows", (SEQ, HG)), scratch("gate_rows_a", (SEQ, HG))
    o_rows = [scratch(f"head_out{d}", (SEQ, HG)) for d in range(2)]
    pieces = {name: scratch(f"piece_{name}", (HG, SEQ)) for name in PIECES}
    y_f = scratch("fourier_out", (FW, SEQ))
    with Room(nc, "all") as r:
        ident = r.sb("ident", [P, P])
        with Room(nc, "hidden") as s:
            masks = s.sb("masks", [P, 2, MASKED, P], U8)
            mod_mul, mod_add = s.sb("mod_mul", [P, KT, 2]), s.sb("mod_add", [P, KT, 2])
            one_minus_lb = s.sb("one_minus_lb", [P, 2, HEADS])
            constants(nc, masks_in, ident, masks)
            modulation(nc, conds, w_ada, b_ada, b_ada_cols, norm_w_cols, bounds_cols, mod_mul, mod_add, one_minus_lb, gate_rows)
            with Room(nc, "c") as t:
                hi, lo = t.sb("h_hi", [P, KT, CTX], F32R), t.sb("h_lo", [P, KT, CTX], F32R)
                hidden(nc, "hc", ctx[0], CTX // P, 1, None, None, mod_mul, mod_add, ident, hi, lo)
                context(nc, w_in, one_minus_lb, ident, hi, lo, states)
            with Room(nc, "x") as t:
                hi, lo = t.sb("h_hi", [P, KT, SEQ], F32R), t.sb("h_lo", [P, KT, SEQ], F32R)
                hidden(nc, "hx", x[0], NT, 0, row_code, col_code, mod_mul, mod_add, ident, hi, lo)
                natural(nc, w_in, hi, lo, value_rows, gate_rows_a)
                first_head(nc, w_in, hi, lo, pieces)
                heads(nc, w_in, one_minus_lb, ident, masks, hi, lo, states, value_rows, pieces, o_rows)
        fourier(nc, tables, chan_tables, sign_cols, sign_row, w_fourier[0].rearrange("g c d -> (g c) d"), b_fourier_cols,
                pieces["wave"], pieces["gate_f"], y_f)
        output(nc, ident, x[0], row_code, col_code, w_out, o_rows, gate_rows_a, y_f, gate_rows, hgrn_cols, final_norm_w, out[0])


def as_columns(v):
    return np.ascontiguousarray(np.asarray(v).reshape(-1, P).T)


def position_codes():
    quarter = D // 4
    omega = np.power(np.float32(10000.0), -np.arange(quarter, dtype=np.float32) / np.float32(quarter))

    def code(n):
        angle = (np.arange(n, dtype=np.float32)[:, None] * omega[None, :]).astype(np.float64)
        return np.concatenate([np.sin(angle), np.cos(angle)], axis=-1).astype(np.float32)

    return code(SEQ // GRID_W), code(GRID_W)


AS_GIVEN = ["x", "ctx", "w_ada", "b_ada", "w_in", "w_fourier", "w_out", "final_norm_w"]


def kernel(**inputs):
    import concourse.bacc as bacc
    from concourse.bass_utils import run_bass_kernel_spmd

    nc = bacc.Bacc("TRN2", target_bir_lowering=False, num_devices=1)
    row_code, col_code = position_codes()
    tables, chan_tables, sign_cols, sign_row = wave_tables()
    given = {name: inputs[name] for name in AS_GIVEN}
    given |= {
        "conds": np.stack([as_columns(inputs["c"]), as_columns(inputs["c_ctx"])], axis=-1),
        "b_ada_cols": as_columns(inputs["b_ada"]),
        "norm_w_cols": as_columns(inputs["norm_w"]),
        "bounds_cols": as_columns(inputs["lower_bounds"]).reshape(P, 2, HEADS),
        "hgrn_cols": as_columns(inputs["hgrn_norm_w"]),
        "b_fourier_cols": as_columns(inputs["b_fourier"]),
        "row_code": row_code, "col_code": col_code, "masks": score_masks(),
        "tables": tables, "chan_tables": chan_tables, "sign_cols": sign_cols, "sign_row": sign_row,
    }
    arrays, args = {}, []
    for name, a in given.items():
        a = np.ascontiguousarray(a)
        arrays[f"in_{name}"] = a
        args.append(nc.dram_tensor(f"in_{name}", a.shape, mybir.dt.from_np(a.dtype), kind="ExternalInput").ap())
    args.append(nc.dram_tensor("out", (1, SEQ, D), F32, kind="ExternalOutput").ap())
    program(nc, *args)
    return run_bass_kernel_spmd(nc, [arrays], core_ids=[0]).results[0]["out"]
```

```python
from contextlib import ExitStack

import concourse.bass as bass
import numpy as np
from concourse import mybir
from concourse.alu_op_type import AluOpType as ALU

F32 = mybir.dt.float32
F32R = mybir.dt.float32r
U8 = mybir.dt.uint8
ACT = mybir.ActivationFunctionType
AX = mybir.AxisListType

P = 128
D = 1024
SEQ = 2048
CTX = 256
GRID_W = 64
KT = D // P
HEADS = 8
HG = HEADS * P
FG = 4
FC = 256
FW = FG * FC
MIX = HG + FW
NT = SEQ // P
GRP = 512
NG = SEQ // GRP
TPG = GRP // P
EPS = 1e-6
F_MIN = 1e-6
COL_I, COL_ZF, COL_ZB, COL_Q, COL_GA, COL_U, COL_GF = (HG * 0, HG, 2 * HG, 3 * HG, 4 * HG, 5 * HG, 5 * HG + FW)
DMA = 16


def mm3(nc, out, st_hi, st_lo, mv_hi, mv_lo, start, stop):
    nc.tensor.matmul(out, st_hi, mv_hi, start=start, stop=False)
    nc.tensor.matmul(out, st_hi, mv_lo, start=False, stop=False)
    return nc.tensor.matmul(out, st_lo, mv_hi, start=False, stop=stop)


def after(n):
    return n + 1


def row_on_all(ap_1d, n):
    return ap_1d.rearrange("(o n) -> o n", o=1).to_broadcast([P, n])


class Room:

    def __init__(self, nc, stage):
        self.nc, self.stage, self.stack, self.sems, self.at_one = nc, stage, ExitStack(), [], []

    def __enter__(self):
        return self

    def __exit__(self, failed, *a):
        if self.sems and not failed:
            with self.nc.Block() as block:

                @block.gpsimd
                def _(pool):
                    for s in self.sems:
                        pool.sem_clear(s)
        self.stack.close()

    def sb(self, name, shape, dt=F32):
        return self.stack.enter_context(self.nc.sbuf_tensor(f"{self.stage}_{name}", shape, dt))

    def ps(self, name, shape=(P, GRP), dt=F32):
        return self.stack.enter_context(self.nc.psum_tensor(f"{self.stage}_{name}", list(shape), dt))

    def sem(self, name, from_zero=False):
        s = self.stack.enter_context(self.nc.semaphore(f"{self.stage}_{name}"))
        self.sems.append(s)
        if not from_zero:
            self.at_one.append(s)
        return s

    def start_at_one(self):
        with self.nc.Block() as block:

            @block.gpsimd
            def _(pool):
                for s in self.at_one:
                    pool.sem_inc(s, 1)




def constants(nc, masks_in, ident, masks):
    with Room(nc, "const") as r:
        wide = r.sb("wide", [P, 2, MASKED, P])
        cleared, ident_done, masks_here, masks_done = (r.sem(n) for n in ("cleared", "ident_done", "masks_here", "masks_done"))
        with nc.Block() as block:

            @block.sync
            def _(sp):
                sp.dma_start(wide[:], masks_in).then_inc(masks_here, DMA)

            @block.gpsimd
            def _(pool):
                pool.memset(ident[:], 0.0).then_inc(cleared, 1)
                pool.wait_ge(cleared, 1)
                pool.affine_select(out=ident[:], in_=ident[:], compare_op=ALU.not_equal, fill=1.0, base=0,
                                   pattern=[[-1, P]], channel_multiplier=1).then_inc(ident_done, 1)

            @block.vector
            def _(v):
                v.wait_ge(masks_here, DMA)
                nc.vector.tensor_copy(masks[:], wide[:]).then_inc(masks_done, 1)


def modulation(nc, conds, w_ada, b_ada, b_ada_cols, norm_w_cols, bounds_cols, ident, mod_mul, mod_add, one_minus_lb, gate_row):
    AB = 3 * D // GRP
    GB = 2 * D // GRP
    with Room(nc, "mod") as r:
        cond = r.sb("cond", [P, KT, 2])
        silu = r.sb("silu", [P, KT, 2])
        w = [r.sb(f"w{i}", [P, KT, GRP]) for i in range(AB)]
        bias = r.sb("bias", [P, 2 * KT])
        gate_bias = r.sb("gate_bias", [1, D])
        rows = r.sb("rows", [2, 2 * D])
        nw = r.sb("nw", [P, KT])
        vec = r.sb("vec", [P, 2 * KT, 2])
        gate = r.sb("gate", [1, D])
        lb_in = r.sb("lb_in", [P, 2, HEADS])
        lb_exp = r.sb("lb_exp", [P, 2, HEADS])
        lb_inv = r.sb("lb_inv", [P, 2, HEADS])
        lb = r.sb("lb", [P, 2, HEADS])
        ps_vec = r.ps("ps_vec", [P, 2 * KT, 2])
        ps_row = [r.ps(f"ps_row{i}", [2, GRP]) for i in range(AB)]
        cond_in, small_in, silu_done, rows_copied = r.sem("cond_in"), r.sem("small_in"), r.sem("silu_done"), r.sem("rows_copied")
        w_in_sem = [r.sem(f"w_in{i}") for i in range(AB)]
        vec_done, row_done, dve, exp_done, gate_out = r.sem("vec_done"), r.sem("row_done"), r.sem("dve"), r.sem("exp_done"), r.sem("gate_out")
        w_view = w_ada[0].rearrange("(k p) n -> p k n", p=P)
        with nc.Block() as block:

            @block.sync
            def _(sp):
                sp.dma_start(cond[:], conds).then_inc(cond_in, DMA)
                for i in range(AB):
                    sp.dma_start(w[i][:], w_view[:, :, i * GRP:(i + 1) * GRP]).then_inc(w_in_sem[i], DMA)
                sp.wait_ge(dve, 9)
                sp.dma_start(gate_row, gate[:]).then_inc(gate_out, DMA)
                sp.wait_ge(gate_out, DMA)

            @block.scalar
            def _(act):
                act.dma_start(bias[:], b_ada_cols[:, 0:2 * KT]).then_inc(small_in, DMA)
                act.dma_start(gate_bias[:], b_ada[0:1, 2 * D:3 * D]).then_inc(small_in, DMA)
                act.dma_start(nw[:], norm_w_cols).then_inc(small_in, DMA)
                act.dma_start(lb_in[:], bounds_cols).then_inc(small_in, DMA)
                act.wait_ge(cond_in, DMA)
                nc.scalar.activation(silu[:], cond[:], ACT.Silu).then_inc(silu_done, 1)
                act.wait_ge(dve, 1)
                nc.scalar.activation(lb_exp[:], lb_exp[:], ACT.Exp).then_inc(exp_done, 1)
                for b in range(GB):
                    act.wait_ge(row_done, b + 1)
                    nc.scalar.activation(rows[:, b * GRP:(b + 1) * GRP], ps_row[b][:], ACT.Copy).then_inc(rows_copied, 1)

            @block.tensor
            def _(pe):
                pe.wait_ge(silu_done, 1)
                for b in range(AB):
                    pe.wait_ge(w_in_sem[b], DMA)
                    for k in range(KT):
                        last = nc.tensor.matmul(ps_row[b][:], silu[:, k, :], w[b][:, k, :], start=k == 0, stop=k == KT - 1)
                    last.then_inc(row_done, 1)
                    if b < GB:
                        pe.wait_ge(rows_copied, b + 1)
                        for m in range(b * GRP // P, (b + 1) * GRP // P):
                            last = nc.tensor.transpose(ps_vec[:, m, :], rows[:, m * P:(m + 1) * P], ident[0:2, 0:2])
                        if b == GB - 1:
                            last.then_inc(vec_done, 1)

            @block.vector
            def _(v):
                v.wait_ge(small_in, 4 * DMA)
                nc.vector.tensor_tensor(lb_exp[:], lb_in[:], lb_in[:], ALU.subtract).then_inc(dve, 1)
                v.wait_ge(exp_done, 1)
                nc.vector.reciprocal(lb_inv[:], lb_exp[:]).then_inc(dve, 1)
                v.wait_ge(dve, 2)
                nc.vector.tensor_tensor(lb[:], lb_exp[:], lb_inv[:], ALU.mult).then_inc(dve, 1)
                v.wait_ge(dve, 3)
                nc.vector.tensor_tensor(lb_inv[:], lb[:], lb[:], ALU.subtract).then_inc(dve, 1)
                v.wait_ge(dve, 4)
                nc.vector.tensor_scalar(one_minus_lb[:], lb_inv[:], -1.0, 1.0, ALU.mult, ALU.add).then_inc(dve, 1)
                v.wait_ge(vec_done, 1)
                nc.vector.tensor_tensor(vec[:], ps_vec[:], bias[:].rearrange("p (n o) -> p n o", o=1).to_broadcast([P, 2 * KT, 2]),
                                        ALU.add).then_inc(dve, 1)
                v.wait_ge(dve, 6)
                nc.vector.tensor_copy(mod_add[:], vec[:, 0:KT, :])
                nc.vector.scalar_tensor_tensor(mod_mul[:], vec[:, KT:2 * KT, :], 1.0,
                                               nw[:].rearrange("p (n o) -> p n o", o=1).to_broadcast([P, KT, 2]),
                                               ALU.add, ALU.mult).then_inc(dve, 1)
                for i in range(2):
                    v.wait_ge(row_done, GB + i + 1)
                    nc.vector.tensor_tensor(gate[:, i * GRP:(i + 1) * GRP], ps_row[GB + i][0:1, :],
                                            gate_bias[:, i * GRP:(i + 1) * GRP], ALU.add).then_inc(dve, 1)


def hidden(nc, stage, src, tiles, stream, row_code, col_code, mod_mul, mod_add, ident, h_hi, h_lo):
    coded = row_code is not None
    H = D // 2
    RING = min(4, tiles)
    TURNS = tiles // RING
    LOADS = 1 + P // GRID_W if coded else 1
    with Room(nc, stage) as r:
        x = [r.sb(f"x{b}", [P, D]) for b in range(RING)]
        row = [r.sb(f"row{b}", [P, H]) for b in range(RING)] if coded else None
        col = r.sb("col", [P, H]) if coded else None
        square = r.sb("square", [P, D])
        h = [r.sb(f"h{b}", [P, KT, P]) for b in range(2)]
        eps = r.sb("eps", [P, 1])
        warm = r.sb("warm", [P, 1])
        stat = [r.sb(f"stat{b}", [P, 3]) for b in range(RING)]
        ps = [[r.ps(f"ps{b}{i}", [P, KT // 2, P]) for i in range(2)] for b in range(2)]
        x_in = [r.sem(f"x_in{b}") for b in range(RING)]
        col_in, eps_set, warmed = r.sem("col_in"), r.sem("eps_set"), r.sem("warmed")
        coded_done, root_done, sq_done, normed = r.sem("coded_done"), r.sem("root_done"), r.sem("sq_done"), r.sem("normed")
        inv_done, turned, modulated, split_hi, split_done = (r.sem(n) for n in
                                                             ("inv_done", "turned", "modulated", "split_hi", "split_done"))

        def ahead(i, b):
            return i + b // RING, b % RING

        def staged_turn(i, last, first_stage, second_stage, third_stage):
            for b in range(RING):
                if not last or b + 2 < RING:
                    first_stage(*ahead(i, b + 2))
                if not last or b + 1 < RING:
                    second_stage(*ahead(i, b + 1))
                third_stage(i, b)

        def over_turns(engine, turn):
            if TURNS > 1:
                with engine.Fori(0, TURNS - 1) as i:
                    turn(i, False)
            turn(TURNS - 1, True)

        r.start_at_one()
        with nc.Block() as block:

            @block.sync
            def _(sp):
                def load(t, b):
                    sp.dma_start(x[b][:], src[bass.ds(t * P, P), :]).then_inc(x_in[b], DMA)
                    if coded:
                        for half in range(P // GRID_W):
                            sp.dma_start(row[b][half * GRID_W:(half + 1) * GRID_W, :],
                                         row_code[bass.ds(t * 2 + half, 1), :].to_broadcast([GRID_W, H])).then_inc(x_in[b], DMA)

                for b in range(RING):
                    load(b, b)
                    if coded and b == 0:
                        for half in range(P // GRID_W):
                            sp.dma_start(col[half * GRID_W:(half + 1) * GRID_W, :], col_code).then_inc(col_in, DMA)
                if TURNS > 1:
                    with sp.Fori(1, TURNS) as i:
                        for b in range(RING):
                            sp.wait_ge(turned, after(i * RING + b - RING + 1))
                            load(i * RING + b, b)

            @block.vector
            def _(v):
                def add_codes(i, b):
                    if coded:
                        v.wait_ge(x_in[b], after((i + 1) * LOADS * DMA))
                        nc.vector.tensor_tensor(x[b][:, 0:H], x[b][:, 0:H], row[b][:], ALU.add)
                        nc.vector.tensor_tensor(x[b][:, H:D], x[b][:, H:D], col[:], ALU.add).then_inc(coded_done, 1)

                def norm(i, b):
                    t = i * RING + b
                    v.wait_ge(root_done, after(t + 1))
                    nc.vector.reciprocal(stat[b][:, 2:3], stat[b][:, 1:2]).then_inc(inv_done, 1)
                    v.wait_ge(inv_done, after(t + 1))
                    nc.vector.tensor_scalar(x[b][:], x[b][:], stat[b][:, 2:3], None, ALU.mult).then_inc(normed, 1)

                def split(i, b):
                    t = i * RING + b
                    at = bass.ds(t * P, P)
                    v.wait_ge(modulated, after(t + 1))
                    nc.vector.tensor_copy(h_hi[:, :, at], h[b % 2][:]).then_inc(split_hi, 1)
                    v.wait_ge(split_hi, after(t + 1))
                    nc.vector.tensor_tensor(h_lo[:, :, at], h[b % 2][:], h_hi[:, :, at].bitcast(F32), ALU.subtract).then_inc(split_done, 1)

                nc.vector.memset(eps[:], EPS).then_inc(eps_set, 1)
                if coded:
                    v.wait_ge(col_in, after(P // GRID_W * DMA))
                add_codes(0, 0)
                add_codes(0, 1)
                norm(0, 0)
                over_turns(v, lambda i, last: staged_turn(i, last, add_codes, norm, split))

            @block.scalar
            def _(act):
                def root(i, b):
                    t = i * RING + b
                    if coded:
                        act.wait_ge(coded_done, after(t + 1))
                    else:
                        act.wait_ge(x_in[b], after((i + 1) * DMA))
                    act.wait_ge(sq_done, after(t))
                    nc.scalar.activation(square[:], x[b][:], ACT.Square, accum_out=stat[b][:, 0:1]).then_inc(sq_done, 1)
                    act.wait_ge(sq_done, after(t + 1))
                    nc.scalar.activation(stat[b][:, 1:2], stat[b][:, 0:1], ACT.Sqrt, scale=1.0 / D, bias=eps[:, 0:1]).then_inc(root_done, 1)

                def modulate(i, b):
                    t = i * RING + b
                    act.wait_ge(turned, after(t + 1))
                    if b >= 2:
                        act.wait_ge(split_done, after(t - 1))
                    else:
                        act.wait_ge(split_done, after(i * RING))
                    for k in range(KT):
                        last = nc.scalar.activation(h[b % 2][:, k, :], ps[b % 2][k // 4][:, k % 4, :], ACT.Identity,
                                                    scale=mod_mul[:, k, stream:stream + 1], bias=mod_add[:, k, stream:stream + 1])
                    last.then_inc(modulated, 1)

                def turn(i, last):
                    act.wait_ge(warmed, after(i))
                    nc.scalar.activation(warm[:], eps[:], ACT.Sqrt).then_inc(warmed, 1)
                    staged_turn(i, last, lambda i, b: None, root, modulate)

                act.wait_ge(eps_set, after(1))
                root(0, 0)
                over_turns(act, turn)

            @block.tensor
            def _(pe):
                def transpose(i, b):
                    t = i * RING + b
                    pe.wait_ge(normed, after(t + 1))
                    if b >= 2:
                        pe.wait_ge(modulated, after(t - 1))
                    else:
                        pe.wait_ge(modulated, after(i * RING))
                    for k in range(KT):
                        last = nc.tensor.transpose(ps[b % 2][k // 4][:, k % 4, :], x[b][:, k * P:(k + 1) * P], ident[:])
                    last.then_inc(turned, 1)

                over_turns(pe, lambda i, last: [transpose(i, b) for b in range(RING)])


def context(nc, w_in, one_minus_lb, ident, h_hi, h_lo, states):
    CT = CTX // P
    TURNS = HEADS // 2
    with Room(nc, "ctx") as r:
        def two(name, shape, dt=F32):
            return [r.sb(f"{name}{s}", shape, dt) for s in range(2)]

        def two_by_direction(name, shape):
            return [[r.sb(f"{name}{s}{d}", shape) for d in range(2)] for s in range(2)]

        PARTS = ((0, 1, 2), (1, 2))

        def weights(name, dt=F32):
            return [{j: r.sb(f"{name}{s}{j}", [P, KT, P if j else 2 * P], dt) for j in PARTS[s]} for s in range(2)]

        raw, hi, lo = weights("raw"), weights("hi", F32R), weights("lo", F32R)
        value, state = two("value", [P, CT, P]), two("state", [P, 2, P])
        key, gate, suffix = two_by_direction("key", [P, CTX]), two_by_direction("gate", [P, CTX]), two_by_direction("suffix", [P, CTX])
        key_t = two_by_direction("key_t", [P, CT, P])
        ones = r.sb("ones", [P, CTX])
        ps_v = r.ps("ps_v", [P, CT, 2 * P])
        ps_z = [r.ps(f"ps_z{d}", [P, CTX]) for d in range(2)]
        ps_kt = [r.ps(f"ps_kt{d}", [P, CT, P]) for d in range(2)]
        ps_s = r.ps("ps_s", [P, 2, P])
        w_here = [{j: r.sem(f"w_here{s}{j}") for j in PARTS[s]} for s in range(2)]
        lo_done = [r.sem(f"lo_done{s}") for s in range(2)]
        s_out = [r.sem(f"s_out{s}") for s in range(2)]
        hi_done, set_once, z_done = (r.sem(n) for n in ("hi_done", "set_once", "z_done"))
        v_copied, sig_done, gate_raw, key_done, scan_done, weighed = (r.sem(n) for n in
                                                            ("v_copied", "sig_done", "gate_raw", "key_done", "scan_done", "weighed"))
        turned, turned_copied, s_done, s_copied = (r.sem(n) for n in ("turned", "turned_copied", "s_done", "s_copied"))
        w_view = w_in[0].rearrange("(k p) n -> p k n", p=P)
        cols = (COL_I, COL_ZF, COL_ZB)
        r.start_at_one()
        with nc.Block() as block:

            @block.sync
            def _(sp):
                def load(i, s):
                    for j in PARTS[s]:
                        sp.wait_ge(lo_done[s], after(len(PARTS[s]) * i))
                        sp.dma_start(raw[s][j][:], w_view[:, :, bass.ds((2 * i + s) * P + cols[j], P if j else 2 * P)]
                                     ).then_inc(w_here[s][j], DMA)

                with sp.Fori(0, TURNS) as i:
                    load(i, 0)
                    load(i, 1)

            @block.scalar
            def _(act):
                def split_high(i, s):
                    for j in PARTS[s]:
                        act.wait_ge(w_here[s][j], after((i + 1) * DMA))
                        nc.scalar.activation(hi[s][j][:], raw[s][j][:], ACT.Copy).then_inc(hi_done, 1)

                def leave_banks(i, s):
                    h = 2 * i + s
                    for d in range(2):
                        act.wait_ge(z_done, after(2 * h + d + 1))
                        nc.scalar.activation(key[s][d][:], ps_z[d][:], ACT.Sigmoid, scale=-1.0).then_inc(sig_done, 1)
                    nc.scalar.activation(value[s][:], ps_v[:, :, s * P:(s + 1) * P], ACT.Copy).then_inc(v_copied, 1)

                def finish(i, s):
                    h = 2 * i + s
                    for d in range(2):
                        act.wait_ge(turned, after(2 * h + d + 1))
                        nc.scalar.activation(key_t[s][d][:], ps_kt[d][:], ACT.Copy).then_inc(turned_copied, 1)
                    act.wait_ge(s_done, after(h + 1))
                    act.wait_ge(s_out[s], after(i * 2 * DMA))
                    nc.scalar.activation(state[s][:], ps_s[:], ACT.Copy).then_inc(s_copied, 1)
                    act.wait_ge(s_copied, after(h + 1))
                    for d in range(2):
                        act.dma_start(states[d][bass.ds(h * P, P), :], state[s][:, d, :]).then_inc(s_out[s], DMA)

                def turn(i, last):
                    leave_banks(i, 1)
                    if not last:
                        split_high(i + 1, 0)
                    finish(i, 0)
                    if not last:
                        leave_banks(i + 1, 0)
                        split_high(i + 1, 1)
                    finish(i, 1)

                split_high(0, 0)
                split_high(0, 1)
                leave_banks(0, 0)
                with act.Fori(0, TURNS - 1) as i:
                    turn(i, False)
                turn(TURNS - 1, True)
                for s in range(2):
                    act.wait_ge(s_out[s], after(TURNS * 2 * DMA))

            @block.tensor
            def _(pe):
                def project(i, s):
                    h = 2 * i + s
                    if s == 0:
                        pe.wait_ge(lo_done[s], after(3 * i + 1))
                        pe.wait_ge(v_copied, after(2 * i))
                        for t in range(CT):
                            for k in range(KT):
                                last = mm3(nc, ps_v[:, t, :], h_hi[:, k, t * P:(t + 1) * P], h_lo[:, k, t * P:(t + 1) * P],
                                           hi[s][0][:, k, :], lo[s][0][:, k, :], k == 0, k == KT - 1)
                    for d in range(2):
                        pe.wait_ge(lo_done[s], after(len(PARTS[s]) * i + PARTS[s].index(d + 1) + 1))
                        pe.wait_ge(sig_done, after(2 * h))
                        for k in range(KT):
                            last = mm3(nc, ps_z[d][:], hi[s][d + 1][:, k, :], lo[s][d + 1][:, k, :], h_hi[:, k, :], h_lo[:, k, :],
                                       k == 0, k == KT - 1)
                        last.then_inc(z_done, 1)

                def finish(i, s):
                    h = 2 * i + s
                    for d in range(2):
                        pe.wait_ge(weighed, after(2 * h + d + 1))
                        pe.wait_ge(turned_copied, after(2 * h))
                        for t in range(CT):
                            last = nc.tensor.transpose(ps_kt[d][:, t, :], key[s][d][:, t * P:(t + 1) * P], ident[:])
                        last.then_inc(turned, 1)
                    pe.wait_ge(v_copied, after(h + 1))
                    pe.wait_ge(s_copied, after(h))
                    for d in range(2):
                        pe.wait_ge(turned_copied, after(2 * h + d + 1))
                        for t in range(CT):
                            last = nc.tensor.matmul(ps_s[:, d, :], key_t[s][d][:, t, :], value[s][:, t, :], start=t == 0, stop=t == CT - 1)
                    last.then_inc(s_done, 1)

                def turn(i, last):
                    project(i, 1)
                    finish(i, 0)
                    if not last:
                        project(i + 1, 0)
                    finish(i, 1)

                project(0, 0)
                with pe.Fori(0, TURNS - 1) as i:
                    turn(i, False)
                turn(TURNS - 1, True)

            @block.vector
            def _(v):
                def split_low(i, s):
                    for n, j in enumerate(PARTS[s]):
                        v.wait_ge(hi_done, after(5 * i + 3 * s + n + 1))
                        nc.vector.tensor_tensor(lo[s][j][:], raw[s][j][:], hi[s][j][:].bitcast(F32), ALU.subtract).then_inc(lo_done[s], 1)

                def weigh(i, s):
                    h = 2 * i + s
                    for d in range(2):
                        v.wait_ge(sig_done, after(2 * h + d + 1))
                        nc.vector.tensor_scalar(key[s][d][:], key[s][d][:], one_minus_lb[:, d, bass.ds(h, 1)], None,
                                                ALU.mult).then_inc(key_done, 1)
                    for d in range(2):
                        v.wait_ge(key_done, after(2 * h + d + 1))
                        nc.vector.tensor_scalar(gate[s][d][:], key[s][d][:], -1.0, 1.0, ALU.mult, ALU.add).then_inc(gate_raw, 1)
                    for d in range(2):
                        v.wait_ge(gate_raw, after(4 * h + d + 1))
                        nc.vector.tensor_scalar(gate[s][d][:], gate[s][d][:], F_MIN, None, ALU.max).then_inc(gate_raw, 1)
                    for d in range(2):
                        v.wait_ge(gate_raw, after(4 * h + 3 + d))
                        if d == 0:
                            out, data = suffix[s][0][:, CTX - 2::-1], gate[s][0][:, CTX - 1:0:-1]
                        else:
                            out, data = suffix[s][1][:, 1:CTX], gate[s][1][:, 0:CTX - 1]
                        nc.vector.tensor_tensor_scan(out, data, ones[:, 0:CTX - 1], 1.0, ALU.mult, ALU.mult).then_inc(scan_done, 1)
                    for d in range(2):
                        v.wait_ge(scan_done, after(2 * h + d + 1))
                        nc.vector.tensor_tensor(key[s][d][:], key[s][d][:], suffix[s][d][:], ALU.mult).then_inc(weighed, 1)

                def turn(i, last):
                    weigh(i, 1)
                    if not last:
                        split_low(i + 1, 0)
                        weigh(i + 1, 0)
                        split_low(i + 1, 1)

                nc.vector.memset(ones[:], 1.0).then_inc(set_once, 1)
                for s in range(2):
                    nc.vector.memset(suffix[s][0][:, CTX - 1:CTX], 1.0).then_inc(set_once, 1)
                    nc.vector.memset(suffix[s][1][:, 0:1], 1.0).then_inc(set_once, 1)
                v.wait_ge(set_once, after(5))
                split_low(0, 0)
                split_low(0, 1)
                weigh(0, 0)
                with v.Fori(0, TURNS - 1) as i:
                    turn(i, False)
                turn(TURNS - 1, True)


def natural(nc, w_in, h_hi, h_lo, value_rows, gate_rows_a):
    W = 256
    STORE = 4
    TURNS = HG // W
    FILLS = NT // 2
    with Room(nc, "nat") as r:
        raw = [r.sb(f"raw{b}", [P, KT, W]) for b in range(2)]
        hi = [r.sb(f"hi{b}", [P, KT, W], F32R) for b in range(2)]
        lo = [r.sb(f"lo{b}", [P, KT, W], F32R) for b in range(2)]
        out = [r.sb(f"out{i}", [P, STORE, W]) for i in range(2)]
        ps = [[r.ps(f"ps{b}{i}", [P, 2, W]) for i in range(4)] for b in range(2)]
        w_here, hi_done, lo_done, product, evacuated = ([r.sem(f"{n}{b}") for b in range(2)] for n in
                                                        ("w_here", "hi_done", "lo_done", "product", "evacuated"))
        stored = [r.sem(f"stored{i}") for i in range(2)]
        w_view = w_in[0].rearrange("(k p) n -> p k n", p=P)
        cols, rows = (COL_I, COL_GA), [m.rearrange("(t p) n -> p t n", p=P) for m in (value_rows, gate_rows_a)]
        funcs = (ACT.Copy, ACT.Silu)
        r.start_at_one()
        with nc.Block() as block:

            @block.sync
            def _(sp):
                with sp.Fori(0, TURNS) as i:
                    for b in range(2):
                        sp.wait_ge(lo_done[b], after(i))
                        sp.dma_start(raw[b][:], w_view[:, :, bass.ds(i * W + cols[b], W)]).then_inc(w_here[b], DMA)

            @block.vector
            def _(v):
                with v.Fori(0, TURNS) as i:
                    for b in range(2):
                        v.wait_ge(w_here[b], after((i + 1) * DMA))
                        v.wait_ge(product[b], after(i * FILLS))
                        nc.vector.tensor_copy(hi[b][:], raw[b][:]).then_inc(hi_done[b], 1)
                        v.wait_ge(hi_done[b], after(i + 1))
                        nc.vector.tensor_tensor(lo[b][:], raw[b][:], hi[b][:].bitcast(F32), ALU.subtract).then_inc(lo_done[b], 1)

            @block.tensor
            def _(pe):
                with pe.Fori(0, TURNS) as i:
                    for b in range(2):
                        pe.wait_ge(lo_done[b], after(i + 1))
                        for fill in range(FILLS):
                            pe.wait_ge(evacuated[b], after(i * FILLS + max(fill - 3, 0)))
                            for u in range(2):
                                t = 2 * fill + u
                                for k in range(KT):
                                    last = mm3(nc, ps[b][fill % 4][:, u, :], h_hi[:, k, t * P:(t + 1) * P],
                                               h_lo[:, k, t * P:(t + 1) * P], hi[b][:, k, :], lo[b][:, k, :], k == 0, k == KT - 1)
                            last.then_inc(product[b], 1)

            @block.scalar
            def _(act):
                with act.Fori(0, TURNS) as i:
                    for b in range(2):
                        for fill in range(FILLS):
                            o, first = fill // 2 % 2, 2 * fill % STORE
                            act.wait_ge(product[b], after(i * FILLS + fill + 1))
                            if first == 0:
                                act.wait_ge(stored[o], after((i * 4 + 2 * b + fill // 4) * DMA))
                            nc.scalar.activation(out[o][:, first:first + 2, :], ps[b][fill % 4][:],
                                                 funcs[b]).then_inc(evacuated[b], 1)
                            if first:
                                act.wait_ge(evacuated[b], after(i * FILLS + fill + 1))
                                t = 2 * fill - first
                                act.dma_start(rows[b][:, t:t + STORE, bass.ds(i * W, W)], out[o][:]).then_inc(stored[o], DMA)
                for o in range(2):
                    act.wait_ge(stored[o], after(TURNS * 4 * DMA))


PIECES = {
    "query": (COL_Q, ACT.Silu, 1.0),
    "key_f": (COL_ZF, ACT.Sigmoid, -1.0),
    "key_b": (COL_ZB, ACT.Sigmoid, -1.0),
    "gate_f": (COL_GF, ACT.Silu, 1.0),
    "wave": (COL_U, ACT.Copy, 1.0),
}
OF_NEXT = ("query", "key_f", "key_b")
OF_THIS = ("gate_f", "wave")


def first_head(nc, w_in, h_hi, h_lo, scratch):
    with Room(nc, "first") as r:
        n = len(OF_NEXT)
        raw = [r.sb(f"raw{j}", [P, KT, P]) for j in range(n)]
        hi = [r.sb(f"hi{j}", [P, KT, P], F32R) for j in range(n)]
        lo = [r.sb(f"lo{j}", [P, KT, P], F32R) for j in range(n)]
        out = [r.sb(f"out{j}", [P, SEQ]) for j in range(2)]
        ps = [r.ps(f"ps{i}") for i in range(4)]
        w_here = [r.sem(f"w_here{j}") for j in range(n)]
        hi_done, lo_done, product, evacuated = (r.sem(s) for s in ("hi_done", "lo_done", "product", "evacuated"))
        stored = [r.sem(f"stored{j}") for j in range(n)]
        w_view = w_in[0].rearrange("(k p) n -> p k n", p=P)
        with nc.Block() as block:

            @block.sync
            def _(sp):
                for j, name in enumerate(OF_NEXT):
                    col = PIECES[name][0]
                    sp.dma_start(raw[j][:], w_view[:, :, col:col + P]).then_inc(w_here[j], DMA)

            @block.vector
            def _(v):
                for j in range(n):
                    v.wait_ge(w_here[j], DMA)
                    nc.vector.tensor_copy(hi[j][:], raw[j][:]).then_inc(hi_done, 1)
                    v.wait_ge(hi_done, j + 1)
                    nc.vector.tensor_tensor(lo[j][:], raw[j][:], hi[j][:].bitcast(F32), ALU.subtract).then_inc(lo_done, 1)

            @block.tensor
            def _(pe):
                for j in range(n):
                    pe.wait_ge(lo_done, j + 1)
                    for g in range(NG):
                        if j:
                            pe.wait_ge(evacuated, (j - 1) * NG + g + 1)
                        for k in range(KT):
                            last = mm3(nc, ps[g][:], hi[j][:, k, :], lo[j][:, k, :], h_hi[:, k, g * GRP:(g + 1) * GRP],
                                       h_lo[:, k, g * GRP:(g + 1) * GRP], k == 0, k == KT - 1)
                        last.then_inc(product, 1)

            @block.scalar
            def _(act):
                for j, name in enumerate(OF_NEXT):
                    if j >= 2:
                        act.wait_ge(stored[j - 2], DMA)
                    for g in range(NG):
                        act.wait_ge(product, j * NG + g + 1)
                        nc.scalar.activation(out[j % 2][:, g * GRP:(g + 1) * GRP], ps[g][:], PIECES[name][1],
                                             scale=PIECES[name][2]).then_inc(evacuated, 1)
                    act.wait_ge(evacuated, (j + 1) * NG)
                    act.dma_start(scratch[name][0:P, :], out[j % 2][:]).then_inc(stored[j], DMA)
                for j in range(n):
                    act.wait_ge(stored[j], DMA)


LEVELS = (1, 2, 4, 8, 16, 32, 64)
MASKED = 6


def score_masks():
    s, t = np.arange(P)[:, None], np.arange(P)[None, :]
    masks = np.zeros((P, 2, MASKED, P), np.float32)
    for d in range(2):
        a, b = (s, t) if d == 0 else (P - 1 - s, P - 1 - t)
        masks[:, d, 0] = a == b
        for i, n in enumerate(LEVELS[:MASKED - 2]):
            masks[:, d, i + 1] = (b // n % 2 == 1) & (a // n == b // n - 1)
        masks[:, d, MASKED - 1] = a // 16 < b // 16
    return masks


def heads(nc, w_in, one_minus_lb, ident, masks, h_hi, h_lo, states, value_rows, scratch, o_rows):
    PROD, OPS, CHAIN, TOT = 11, 9, 5, 7
    KEYS_T, INC, OUT = 9, 10, 11
    PIECE_SLOT = (0, 1, 0, 1, 0)
    HALVES = 2 * NG * len(PIECE_SLOT)
    PER_STEP = HALVES // NG
    with Room(nc, "head") as r:
        raw = r.sb("raw", [P, KT, P])
        hi = [r.sb(f"hi{b}", [P, KT, P], F32R) for b in range(2)]
        lo = [r.sb(f"lo{b}", [P, KT, P], F32R) for b in range(2)]
        projected = [r.sb(f"projected{b}", [P, GRP]) for b in range(2)]
        query = [[r.sb(f"query{d}{b}", [P, GRP]) for b in range(2)] for d in range(2)]
        key = [[r.sb(f"key{d}{b}", [P, GRP]) for b in range(2)] for d in range(2)]
        value = [[r.sb(f"value{d}{b}", [P, TPG, P]) for b in range(2)] for d in range(2)]
        gate = [r.sb(f"gate{d}", [P, GRP]) for d in range(2)]
        total = [r.sb(f"total{d}", [P, GRP]) for d in range(2)]
        score = [r.sb(f"score{d}", [P, TPG, P]) for d in range(2)]
        key_t = [r.sb(f"key_t{d}", [P, TPG, P]) for d in range(2)]
        state = [r.sb(f"state{d}", [P, TPG + 1, P]) for d in range(2)]
        o = [r.sb(f"o{d}", [P, TPG, P]) for d in range(2)]
        ps_proj = [r.ps(f"ps_proj{b}") for b in range(2)]
        ps = [[r.ps(f"ps{d}{i}", [P, TPG, P]) for i in range(3)] for d in range(2)]
        w_here = r.sem("w_here", from_zero=True)
        hi_done, lo_done = r.sem("hi_done"), r.sem("lo_done")
        proj_done, proj_copied = r.sem("proj_done"), r.sem("proj_copied")
        proj_stored = [r.sem(f"proj_stored{b}") for b in range(2)]
        loaded = [[r.sem(f"loaded{d}{b}") for b in range(2)] for d in range(2)]
        cleared = r.sem("cleared")
        product = [r.sem(f"product{d}") for d in range(2)]
        operand = [r.sem(f"operand{d}") for d in range(2)]
        gated = [r.sem(f"gated{d}") for d in range(2)]
        totalled = [r.sem(f"totalled{d}") for d in range(2)]
        copied = [r.sem(f"copied{d}") for d in range(2)]
        chained = [r.sem(f"chained{d}") for d in range(2)]
        start_here = [r.sem(f"start_here{d}") for d in range(2)]
        key_t_copied = [r.sem(f"key_t_copied{d}") for d in range(2)]
        o_copied = [r.sem(f"o_copied{d}") for d in range(2)]
        o_stored = [r.sem(f"o_stored{d}") for d in range(2)]
        w_view = w_in[0].rearrange("(k p) n -> p k n", p=P)
        key_names = ("key_f", "key_b")
        LOADS = 3

        def meeting(ap, d, size):
            lead = "p t" if len(ap.shape) == 3 else "p"
            both = ap.rearrange(f"{lead} (n two b) -> {lead} n two b", two=2, b=size)
            return both[:, :, :, 1 - d, :] if len(ap.shape) == 3 else both[:, :, 1 - d, :]

        def group_of(d, g):
            return g if d == 0 else NG - 1 - g

        def in_time(ap, d):
            return ap if d == 0 else ap[:, ::-1]

        def total_of(d, b):
            if b == 1:
                return in_time(gate[d][:], d)
            at = GRP - 2 * GRP // b
            return total[d][:, at:at + GRP // b]

        def pieces(h, last):
            return ([] if last else [(name, h + 1) for name in OF_NEXT]) + [(name, h) for name in OF_THIS]

        def halves_at(g, slot, last):
            n = g * PER_STEP + slot
            return n if n < 2 * NG * len(pieces(0, last)) else None

        def slot_of(j, last):
            return PIECE_SLOT[j + (len(OF_NEXT) if last else 0)]

        r.start_at_one()
        with nc.Block() as block:

            @block.gpsimd
            def _(pool):
                for d in range(2):
                    pool.memset(score[d][:], 0.0).then_inc(cleared, 1)

                def turn(h, last):
                    for j, (name, head) in enumerate(pieces(h, last)):
                        pool.wait_ge(lo_done, after(5 * h + j))
                        pool.dma_start(raw[:], w_view[:, :, bass.ds(PIECES[name][0] + head * P, P)]).then_inc(w_here, DMA)

                with pool.Fori(0, HEADS - 1) as h:
                    turn(h, False)
                turn(HEADS - 1, True)

            @block.sync
            def _(sp):
                def start_state(h):
                    for d in range(2):
                        sp.wait_ge(chained[d], after(CHAIN * NG * h))
                        sp.dma_start(state[d][:, TPG, :], states[d][bass.ds(h * P, P), :]).then_inc(start_here[d], DMA)

                def load(h, g):
                    for d in range(2):
                        t = group_of(d, g) * GRP
                        sem, b = loaded[d][g % 2], g % 2
                        sp.dma_start(query[d][b][:], scratch["query"][bass.ds(h * P, P), t:t + GRP]).then_inc(sem, DMA)
                        sp.dma_start(key[d][b][:], scratch[key_names[d]][bass.ds(h * P, P), t:t + GRP]).then_inc(sem, DMA)
                        sp.dma_start(value[d][b][:], value_rows[t:t + GRP, bass.ds(h * P, P)].rearrange("(t p) n -> p t n", p=P)
                                     ).then_inc(sem, DMA)

                def turn(h, last):
                    start_state(h)
                    for g in range(NG):
                        if g == NG - 1 and last:
                            break
                        for d in range(2):
                            sp.wait_ge(product[d], after(PROD * (NG * h + g)))
                        if g < NG - 1:
                            load(h, g + 1)
                        else:
                            for b in range(2):
                                sp.wait_ge(proj_stored[b], after((10 * h + 6) * DMA))
                            load(h + 1, 0)

                load(0, 0)
                with sp.Fori(0, HEADS - 1) as h:
                    turn(h, False)
                turn(HEADS - 1, True)

            @block.tensor
            def _(pe):
                def project_half(h, last, g, slot):
                    n = halves_at(g, slot, last)
                    if n is None:
                        return
                    unit, half = n // 2, n % 2
                    j, group = unit // NG, unit % NG
                    b = slot_of(j, last)
                    if group == 0 and half == 0:
                        pe.wait_ge(lo_done, after(5 * h + j + 1))
                    if half == 0:
                        if unit < 2:
                            pe.wait_ge(proj_copied, after(20 * h))
                        else:
                            pe.wait_ge(proj_copied, after(20 * h + unit - 1))
                    for k in range(half * KT // 2, (half + 1) * KT // 2):
                        done = mm3(nc, ps_proj[unit % 2][:], hi[b][:, k, :], lo[b][:, k, :],
                                   h_hi[:, k, group * GRP:(group + 1) * GRP], h_lo[:, k, group * GRP:(group + 1) * GRP],
                                   k == 0, k == KT - 1)
                    if half == 1:
                        done.then_inc(proj_done, 1)

                def tile(ap, t):
                    return ap[:, t * P:(t + 1) * P]

                def step(h, g, last):
                    n, b = NG * h + g, g % 2
                    for d in range(2):
                        pe.wait_ge(loaded[d][b], after((2 * h + g // 2 + 1) * LOADS * DMA))
                        pe.wait_ge(operand[d], after(OPS * n + 1))
                        for t in range(TPG):
                            done = nc.tensor.matmul(ps[d][0][:, t, :], tile(key[d][b], t), tile(query[d][b], t), start=True, stop=True)
                        done.then_inc(product[d], 1)
                    project_half(h, last, g, 0)
                    for i in range(5):
                        for d in range(2):
                            pe.wait_ge(operand[d], after(OPS * n + 2 + i))
                            if i == 0:
                                pe.wait_ge(chained[d], after(CHAIN * n))
                            elif i == 1:
                                pe.wait_ge(o_copied[d], after(n))
                            else:
                                pe.wait_ge(copied[d], after(MASKED * n + i - 1))
                            for t in range(TPG):
                                done = nc.tensor.matmul(meeting(ps[d][(i + 1) % 3][:, t, :], d, LEVELS[i]), tile(key[d][b], t),
                                                        meeting(tile(query[d][b], t), d, LEVELS[i]), start=True, stop=True)
                            done.then_inc(product[d], 1)
                        project_half(h, last, g, 1 + i)
                    for i, size in ((5, 32), (6, 64)):
                        for d in range(2):
                            pe.wait_ge(operand[d], after(OPS * n + 2 + i))
                            for t in range(TPG):
                                for pair in range(P // (2 * size)):
                                    s, q = (2 * pair, 2 * pair + 1) if d == 0 else (2 * pair + 1, 2 * pair)
                                    s, q = slice(s * size, (s + 1) * size), slice(q * size, (q + 1) * size)
                                    done = nc.tensor.matmul(ps[d][2][s, t, q], tile(key[d][b], t)[:, s], tile(query[d][b], t)[:, q],
                                                            start=True, stop=True)
                            done.then_inc(product[d], 1)
                        project_half(h, last, g, 1 + i)
                    for d in range(2):
                        pe.wait_ge(operand[d], after(OPS * n + OPS))
                        pe.wait_ge(copied[d], after(MASKED * n + 4))
                        for t in range(TPG):
                            done = nc.tensor.transpose(ps[d][0][:, t, :], tile(key[d][b], t), ident[:])
                        done.then_inc(product[d], 1)
                    project_half(h, last, g, 8)
                    for d in range(2):
                        pe.wait_ge(key_t_copied[d], after(n + 1))
                        pe.wait_ge(copied[d], after(MASKED * n + 5))
                        for t in range(TPG):
                            done = nc.tensor.matmul(ps[d][1][:, t, :], key_t[d][:, t, :], value[d][b][:, t, :], start=True, stop=True)
                        done.then_inc(product[d], 1)
                    project_half(h, last, g, 9)
                    for d in range(2):
                        pe.wait_ge(copied[d], after(MASKED * n + MASKED))
                        pe.wait_ge(chained[d], after(CHAIN * n + TPG))
                        for t in range(TPG):
                            before = t if d == 0 else TPG - 1 - t
                            nc.tensor.matmul(ps[d][2][:, t, :], score[d][:, t, :], value[d][b][:, t, :], start=True, stop=False)
                            done = nc.tensor.matmul(ps[d][2][:, t, :], tile(query[d][b], t), state[d][:, before, :], start=False, stop=True)
                        done.then_inc(product[d], 1)

                pe.wait_ge(cleared, 5)
                with pe.Fori(0, HEADS - 1) as h:
                    for g in range(NG):
                        step(h, g, False)
                for g in range(NG):
                    step(HEADS - 1, g, True)

            @block.scalar
            def _(act):
                def split_high(h, j, last):
                    act.wait_ge(w_here, (5 * h + j + 1) * DMA)
                    free = freed_units(h, j, last)
                    act.wait_ge(proj_done, after(free))
                    nc.scalar.activation(hi[slot_of(j, last)][:], raw[:], ACT.Copy).then_inc(hi_done, 1)

                def freed_units(h, j, last):
                    if j == 0:
                        return 20 * h
                    return 20 * h + NG * (j - 1) if not last or j > 1 else 20 * h

                def evacuate(h, last, g, slot):
                    n = halves_at(g, slot, last)
                    if n is None or n % 2 == 0:
                        return
                    unit = n // 2
                    j, group = unit // NG, unit % NG
                    name, head = pieces(h, last)[j]
                    act.wait_ge(proj_done, after(20 * h + unit + 1))
                    act.wait_ge(proj_stored[unit % 2], after((10 * h + unit // 2) * DMA))
                    nc.scalar.activation(projected[unit % 2][:], ps_proj[unit % 2][:], PIECES[name][1],
                                         scale=PIECES[name][2]).then_inc(proj_copied, 1)
                    act.wait_ge(proj_copied, after(20 * h + unit + 1))
                    act.dma_start(scratch[name][bass.ds(head * P, P), group * GRP:(group + 1) * GRP],
                                  projected[unit % 2][:]).then_inc(proj_stored[unit % 2], DMA)
                    if group == 0 and j + 1 < len(pieces(h, last)):
                        split_high(h, j + 1, last)

                def step(h, g, last):
                    n = NG * h + g
                    for slot in range(9):
                        evacuate(h, last, g, slot)
                    for d in range(2):
                        act.wait_ge(product[d], after(PROD * n + KEYS_T))
                        nc.scalar.activation(key_t[d][:], ps[d][0][:], ACT.Copy).then_inc(key_t_copied[d], 1)
                    evacuate(h, last, g, 9)
                    for d in range(2):
                        act.wait_ge(product[d], after(PROD * n + OUT))
                        act.wait_ge(o_stored[d], after(n * DMA))
                        nc.scalar.activation(o[d][:], ps[d][2][:], ACT.Copy).then_inc(o_copied[d], 1)
                    for d in range(2):
                        act.wait_ge(o_copied[d], after(n + 1))
                        t = group_of(d, g) * GRP
                        act.dma_start(o_rows[d][t:t + GRP, bass.ds(h * P, P)].rearrange("(t p) n -> p t n", p=P),
                                      o[d][:]).then_inc(o_stored[d], DMA)

                def turn(h, last):
                    split_high(h, 0, last)
                    for g in range(NG):
                        step(h, g, last)

                with act.Fori(0, HEADS - 1) as h:
                    turn(h, False)
                turn(HEADS - 1, True)
                for b in range(2):
                    act.wait_ge(proj_stored[b], after((10 * (HEADS - 1) + NG * len(OF_THIS) // 2) * DMA))
                for d in range(2):
                    act.wait_ge(o_stored[d], after(NG * HEADS * DMA))

            @block.vector
            def _(v):
                def split_low(h, j, last):
                    v.wait_ge(hi_done, after(5 * h + j + 1))
                    b = slot_of(j, last)
                    nc.vector.tensor_tensor(lo[b][:], raw[:], hi[b][:].bitcast(F32), ALU.subtract).then_inc(lo_done, 1)

                def split_due(g, level, last):
                    for j in range(0, len(pieces(0, last)) - 1):
                        half = 2 * NG * j + 2
                        if (half // PER_STEP, max(1, min(half % PER_STEP, 7))) == (g, level):
                            return j + 1
                    return None

                def copy_scores(d, c, bank):
                    dst, mask, src = score[d][:], masks[:, d, c:c + 1, :], ps[d][bank][:]
                    if 0 < c < MASKED - 1:
                        dst, mask, src = (meeting(ap, d, LEVELS[c - 1]) for ap in (dst, mask, src))
                    nc.vector.copy_predicated(dst, mask.to_broadcast(list(dst.shape)), src).then_inc(copied[d], 1)

                def step(h, g, last):
                    n, b = NG * h + g, g % 2
                    for d in range(2):
                        v.wait_ge(loaded[d][b], after((2 * h + g // 2 + 1) * LOADS * DMA))
                        nc.vector.tensor_scalar(key[d][b][:], key[d][b][:], one_minus_lb[:, d, bass.ds(h, 1)], None,
                                                ALU.mult).then_inc(operand[d], 1)
                    for d in range(2):
                        v.wait_ge(operand[d], after(OPS * n + 1))
                        nc.vector.tensor_scalar(gate[d][:], key[d][b][:], -1.0, 1.0, ALU.mult, ALU.add).then_inc(gated[d], 1)
                    for d in range(2):
                        v.wait_ge(gated[d], after(2 * n + 1))
                        nc.vector.tensor_scalar(gate[d][:], gate[d][:], F_MIN, None, ALU.max).then_inc(gated[d], 1)
                    for d in range(2):
                        v.wait_ge(gated[d], after(2 * n + 2))
                        v.wait_ge(product[d], after(PROD * n + 1))
                        nc.vector.tensor_tensor(query[d][b][:], query[d][b][:], gate[d][:], ALU.mult).then_inc(operand[d], 1)
                    for d in range(2):
                        copy_scores(d, 0, 0)
                    for i, size in enumerate(LEVELS):
                        for d in range(2):
                            blocks = "p (n two b) -> p n two b"
                            qs = in_time(query[d][b][:], d).rearrange(blocks, two=2, b=size)
                            ks = in_time(key[d][b][:], d).rearrange(blocks, two=2, b=size)
                            tot = total_of(d, size).rearrange("p (n two o) -> p n two o", two=2, o=1)
                            shape = [P, GRP // (2 * size), size]
                            v.wait_ge(product[d], after(PROD * n + 2 + i))
                            v.wait_ge(operand[d], after(OPS * n + 2 + i))
                            if i:
                                v.wait_ge(totalled[d], after(TOT * n + i))
                            nc.vector.tensor_tensor(qs[:, :, 1, :], qs[:, :, 1, :], tot[:, :, 0, :].to_broadcast(shape), ALU.mult)
                            nc.vector.tensor_tensor(ks[:, :, 0, :], ks[:, :, 0, :], tot[:, :, 1, :].to_broadcast(shape),
                                                    ALU.mult).then_inc(operand[d], 1)
                            v.wait_ge(copied[d], after(MASKED * n + min(i + 1, MASKED - 1)))
                            nc.vector.tensor_tensor(total_of(d, 2 * size), tot[:, :, 0, 0], tot[:, :, 1, 0],
                                                    ALU.mult).then_inc(totalled[d], 1)
                        if i < MASKED - 2:
                            for d in range(2):
                                copy_scores(d, i + 1, (i + 1) % 3)
                        due = split_due(g, i + 1, last)
                        if due is not None:
                            split_low(h, due, last)
                    for d in range(2):
                        copy_scores(d, MASKED - 1, 2)
                    for d in range(2):
                        v.wait_ge(chained[d], after(CHAIN * n))
                        if g == 0:
                            v.wait_ge(start_here[d], after((h + 1) * DMA))
                        v.wait_ge(product[d], after(PROD * n + 1))
                        nc.vector.tensor_copy(state[d][:, 0, :], state[d][:, TPG, :]).then_inc(chained[d], 1)
                    for j in range(TPG):
                        for d in range(2):
                            t = j if d == 0 else TPG - 1 - j
                            v.wait_ge(chained[d], after(CHAIN * n + j + 1))
                            if j == 0:
                                v.wait_ge(product[d], after(PROD * n + INC))
                                v.wait_ge(totalled[d], after(TOT * n + TOT))
                            nc.vector.scalar_tensor_tensor(state[d][:, j + 1, :], state[d][:, j, :], total_of(d, P)[:, j:j + 1],
                                                           ps[d][1][:, t, :], ALU.mult, ALU.add).then_inc(chained[d], 1)

                def turn(h, last):
                    split_low(h, 0, last)
                    for g in range(NG):
                        step(h, g, last)

                for d in range(2):
                    nc.vector.memset(ps[d][2][:], 0.0).then_inc(cleared, 1)
                v.wait_ge(cleared, 5)
                with v.Fori(0, HEADS - 1) as h:
                    turn(h, False)
                turn(HEADS - 1, True)


HALF, QUART = SEQ // 2, SEQ // 4
QT = QUART // P


def wave_tables():
    t, m = np.arange(QUART, dtype=np.int64)[:, None], np.arange(QUART, dtype=np.int64)[None, :]
    turn = lambda k: 2 * np.pi * (t * k % SEQ) / SEQ
    tab = np.stack([np.cos(turn(2 * m)), np.cos(turn(2 * m + 1)), np.sin(turn(2 * m)), np.sin(turn(2 * m + 1))])
    tab[3, 0] = (-1.0) ** m[0]
    c = np.arange(FC, dtype=np.int64)
    ang = 2 * np.pi * (c[:, None] * c[None, :] % FC) / FC
    chan = np.stack([np.cos(ang), np.sin(ang)]) / np.sqrt(SEQ * FC)
    sign = (-1.0) ** np.arange(QUART)
    return (tab.reshape(4, QT, P, QUART).transpose(2, 0, 1, 3).astype(np.float32),
            chan.reshape(2, 2, P, FC).transpose(2, 0, 1, 3).astype(np.float32),
            np.broadcast_to(sign.reshape(QT, P).T[:, :, None], (P, QT, 2)).astype(np.float32),
            sign[None, :].astype(np.float32))


def fourier(nc, tables_in, chan_in, sign_cols_in, sign_row_in, w_fourier, b_cols_in, wave, gate_f, y_f):
    CC = FC // P
    with Room(nc, "four") as r:
        tab_hi = [r.sb(f"tab_hi{a}", [P, QT, QUART], F32R) for a in range(4)]
        tab_lo = [r.sb(f"tab_lo{a}", [P, QT, QUART], F32R) for a in range(4)]
        sign_cols = r.sb("sign_cols", [P, QT, 2], F32R)
        sign_row = r.sb("sign_row", [1, QUART])
        b_cols = r.sb("b_cols", [P, FW // P])
        chan = r.sb("chan", [P, 2, CC, FC])
        with Room(nc, "tab") as s:
            raw = [s.sb(f"raw{a}", [P, QT, QUART]) for a in range(4)]
            raw_sign = s.sb("raw_sign", [P, QT, 2])
            here, small_here = [s.sem(f"here{a}") for a in range(4)], s.sem("small_here")
            hi_done, lo_done = s.sem("hi_done"), s.sem("lo_done")
            with nc.Block() as block:

                @block.sync
                def _(sp):
                    for a in range(4):
                        sp.dma_start(raw[a][:], tables_in[:, a]).then_inc(here[a], DMA)
                    for dst, src in ((raw_sign, sign_cols_in), (sign_row, sign_row_in), (b_cols, b_cols_in), (chan, chan_in)):
                        sp.dma_start(dst[:], src).then_inc(small_here, DMA)
                    sp.wait_ge(small_here, 4 * DMA)

                @block.scalar
                def _(act):
                    for a in range(4):
                        act.wait_ge(here[a], DMA)
                        nc.scalar.activation(tab_hi[a][:], raw[a][:], ACT.Copy).then_inc(hi_done, 1)
                    act.wait_ge(small_here, 4 * DMA)
                    nc.scalar.activation(sign_cols[:], raw_sign[:], ACT.Copy).then_inc(hi_done, 1)

                @block.vector
                def _(v):
                    for a in range(4):
                        v.wait_ge(hi_done, a + 1)
                        nc.vector.tensor_tensor(tab_lo[a][:], raw[a][:], tab_hi[a][:].bitcast(F32), ALU.subtract).then_inc(lo_done, 1)

        u = r.sb("u", [P, CC, SEQ])
        once = [r.sb(f"once{i}", [P, CC, HALF + 1]) for i in range(2)]
        fold_hi, fold_lo = r.sb("fold_hi", [P, CC, SEQ], F32R), r.sb("fold_lo", [P, CC, SEQ], F32R)
        w = r.sb("w", [P, CC, FC])
        cw = r.sb("cw", [P, CC, FC])
        cw_hi, cw_lo = r.sb("cw_hi", [P, 2, CC, FC], F32R), r.sb("cw_lo", [P, 2, CC, FC], F32R)
        mid = r.sb("mid", [1, FC])
        p_hi = [r.sb(f"p_hi{a}", [P, QT, FC], F32R) for a in range(4)]
        p_lo = [r.sb(f"p_lo{a}", [P, QT, FC], F32R) for a in range(4)]
        sine = r.sb("sine", [P, 2, QUART])
        y = r.sb("y", [P, SEQ])
        g = [r.sb(f"g{c}", [P, SEQ]) for c in range(CC)]
        ps_y = [r.ps(f"ps_y{a}") for a in range(4)]
        ps_p = [r.ps(f"ps_p{i}", [P, 2, FC]) for i in range(2)]
        ps_w = [r.ps(f"ps_w{i}", [P, CC, FC]) for i in range(2)]
        u_here, w_here = r.sem("u_here"), r.sem("w_here")
        g_here, stored = [r.sem(f"g_here{c}") for c in range(CC)], [r.sem(f"stored{c}") for c in range(CC)]
        once_done, fold_done, fold_hi_done, fold_lo_done = (r.sem(n) for n in ("once_done", "fold_done", "fold_hi_done", "fold_lo_done"))
        w_done, w_hi_done, w_lo_done, mid_done, mid_copied = (r.sem(n) for n in ("w_done", "w_hi_done", "w_lo_done", "mid_done", "mid_copied"))
        p_done, p_hi_done, p_lo_done = (r.sem(n) for n in ("p_done", "p_hi_done", "p_lo_done"))
        y_done, sine_copied, combined, top_done, top_copied, gated = (r.sem(n) for n in
                                                                     ("y_done", "sine_copied", "combined", "top_done", "top_copied", "gated"))
        set_once = r.sem("set_once")

        def array(ap, a):
            return ap[:, :, a * QUART:(a + 1) * QUART]

        r.start_at_one()
        with nc.Block() as block:

            @block.sync
            def _(sp):
                def load_u(at):
                    sp.dma_start(u[:], wave[bass.ds(at, FC), :].rearrange("(c p) t -> p c t", p=P)).then_inc(u_here, DMA)

                def load_w(at):
                    sp.dma_start(w[:], w_fourier[bass.ds(at, FC), :].rearrange("(c p) d -> p c d", p=P)).then_inc(w_here, DMA)

                def load_g(at, c):
                    sp.dma_start(g[c][:], gate_f[bass.ds(at, P), :]).then_inc(g_here[c], DMA)

                def turn(n, last):
                    at = [n * FC + c * P for c in range(CC)] if last else [sp.snap(n * FC + c * P) for c in range(CC)]
                    ahead = None if last else [sp.snap(n * FC + FC + c * P) for c in range(CC)]
                    if not last:
                        sp.wait_ge(fold_lo_done, after(n + 1))
                        load_u(ahead[0])
                        sp.wait_ge(w_done, after(2 * n + 2))
                        load_w(ahead[0])
                    for c in range(CC):
                        sp.wait_ge(gated, after(2 * n + c + 1))
                        sp.dma_start(y_f[bass.ds(at[c], P), :], g[c][:]).then_inc(stored[c], DMA)
                        if not last:
                            sp.wait_ge(stored[c], after((n + 1) * DMA))
                            load_g(ahead[c], c)

                load_u(0)
                load_w(0)
                for c in range(CC):
                    load_g(c * P, c)
                with sp.Fori(0, FG - 1) as n:
                    turn(n, False)
                turn(FG - 1, True)
                for c in range(CC):
                    sp.wait_ge(stored[c], after(FG * DMA))

            @block.vector
            def _(v):
                def fold(n):
                    v.wait_ge(u_here, after((n + 1) * DMA))
                    nc.vector.tensor_tensor(once[0][:, :, 1:HALF], u[:, :, 1:HALF], u[:, :, SEQ - 1:HALF:-1], ALU.add)
                    nc.vector.tensor_tensor(once[1][:, :, 1:HALF], u[:, :, 1:HALF], u[:, :, SEQ - 1:HALF:-1], ALU.subtract)
                    nc.vector.tensor_copy(once[0][:, :, 0:HALF + 1:HALF], u[:, :, 0:HALF + 1:HALF]).then_inc(once_done, 1)
                    v.wait_ge(once_done, after(n + 1))
                    for a, op in enumerate((ALU.add, ALU.subtract, ALU.subtract, ALU.add)):
                        src = once[a // 2]
                        nc.vector.tensor_tensor(array(u, a), src[:, :, 0:QUART], src[:, :, HALF:QUART:-1], op).then_inc(fold_done, 1)
                    v.wait_ge(fold_done, after(5 * n + 4))
                    nc.vector.tensor_copy(u[:, :, 3 * QUART:3 * QUART + 1], once[1][:, :, QUART:QUART + 1]).then_inc(fold_done, 1)

                def split_fold_low(n):
                    v.wait_ge(fold_hi_done, after(n + 1))
                    nc.vector.tensor_tensor(fold_lo[:], u[:], fold_hi[:].bitcast(F32), ALU.subtract).then_inc(fold_lo_done, 1)

                def turn(n, last):
                    for i in range(2):
                        v.wait_ge(w_hi_done, after(2 * n + i + 1))
                        nc.vector.tensor_tensor(cw_lo[:, i], ps_w[i][:], cw_hi[:, i].bitcast(F32), ALU.subtract).then_inc(w_lo_done, 1)
                    for f in range(8):
                        a, t = f // 2, f % 2 * 2
                        v.wait_ge(p_hi_done, after(8 * n + f + 1))
                        nc.vector.tensor_tensor(p_lo[a][:, t:t + 2, :], ps_p[f % 2][:], p_hi[a][:, t:t + 2, :].bitcast(F32),
                                                ALU.subtract).then_inc(p_lo_done, 1)
                    if not last:
                        fold(n + 1)
                    for c in range(CC):
                        m = 2 * n + c
                        for odd in range(2):
                            v.wait_ge(sine_copied, after(2 * m + odd + 1))
                            v.wait_ge(y_done, after(4 * m + 2 * odd + 1))
                            v.wait_ge(gated, after(m))
                            cos, sin = ps_y[odd], sine[:, odd, :]
                            nc.vector.tensor_tensor(y[:, odd:HALF:2], cos[:], sin, ALU.subtract)
                            if odd:
                                out, cut = y[:, SEQ - 1:HALF:-2], 0
                            else:
                                out, cut = y[:, SEQ - 2:HALF:-2], 1
                            nc.vector.tensor_tensor(out, cos[:, cut:], sin[:, cut:], ALU.add).then_inc(combined, 1)
                        v.wait_ge(combined, after(2 * m + 2))
                        v.wait_ge(top_copied, after(m + 1))
                        v.wait_ge(g_here[c], after((n + 1) * DMA))
                        nc.vector.scalar_tensor_tensor(g[c][:], y[:], b_cols[:, bass.ds(2 * n + c, 1)], g[c][:],
                                                       ALU.add, ALU.mult).then_inc(gated, 1)
                        if c == 0 and not last:
                            split_fold_low(n + 1)

                nc.vector.memset(once[1][:, :, 0:1], 0.0)
                nc.vector.memset(once[1][:, :, HALF:HALF + 1], 0.0).then_inc(set_once, 1)
                v.wait_ge(set_once, 2)
                fold(0)
                split_fold_low(0)
                with v.Fori(0, FG - 1) as n:
                    turn(n, False)
                turn(FG - 1, True)

            @block.scalar
            def _(act):
                def split_fold(n):
                    act.wait_ge(fold_done, after(5 * n + 5))
                    act.wait_ge(p_done, after(8 * n))
                    nc.scalar.activation(fold_hi[:], u[:], ACT.Copy).then_inc(fold_hi_done, 1)

                def turn(n, last):
                    for i in range(2):
                        act.wait_ge(w_done, after(2 * n + i + 1))
                        act.wait_ge(p_done, after(8 * n))
                        if i == 0:
                            nc.scalar.activation(cw[:], ps_w[0][:], ACT.Copy).then_inc(mid_copied, 1)
                        nc.scalar.activation(cw_hi[:, i], ps_w[i][:], ACT.Copy).then_inc(w_hi_done, 1)
                    act.wait_ge(mid_done, after(n + 1))
                    act.wait_ge(y_done, after(8 * n))
                    nc.scalar.activation(mid[0:1, :], ps_w[0][0:1, 0, :], ACT.Copy).then_inc(mid_copied, 1)
                    for f in range(8):
                        a, t = f // 2, f % 2 * 2
                        act.wait_ge(p_done, after(8 * n + f + 1))
                        act.wait_ge(top_done, after(2 * n))
                        nc.scalar.activation(p_hi[a][:, t:t + 2, :], ps_p[f % 2][:], ACT.Copy).then_inc(p_hi_done, 1)
                    for c in range(CC):
                        m = 2 * n + c
                        for odd in range(2):
                            act.wait_ge(y_done, after(4 * m + 2 * odd + 2))
                            act.wait_ge(combined, after(2 * m))
                            nc.scalar.activation(sine[:, odd, :], ps_y[2 + odd][:], ACT.Copy).then_inc(sine_copied, 1)
                        act.wait_ge(top_done, after(m + 1))
                        act.wait_ge(gated, after(m))
                        nc.scalar.activation(y[:, HALF:HALF + 1], ps_w[1][:, 0, 0:1], ACT.Copy).then_inc(top_copied, 1)
                        if c == 0 and not last:
                            split_fold(n + 1)

                split_fold(0)
                with act.Fori(0, FG - 1) as n:
                    turn(n, False)
                turn(FG - 1, True)

            @block.tensor
            def _(pe):
                with pe.Fori(0, FG) as n:
                    pe.wait_ge(w_here, after((n + 1) * DMA))
                    pe.wait_ge(top_copied, after(2 * n))
                    for i in range(2):
                        for m in range(CC):
                            for k in range(CC):
                                done = nc.tensor.matmul(ps_w[i][:, m, :], chan[:, i, k, m * P:(m + 1) * P], w[:, k, :],
                                                        start=k == 0, stop=k == CC - 1)
                        done.then_inc(w_done, 1)
                    pe.wait_ge(mid_copied, after(2 * n + 1))
                    pe.wait_ge(w_lo_done, after(2 * n + 2))
                    pe.wait_ge(fold_lo_done, after(n + 1))
                    for k in range(CC):
                        done = nc.tensor.matmul(ps_w[0][0:1, 0, :], once[0][:, k, QUART:QUART + 1], cw[:, k, :],
                                                start=k == 0, stop=k == CC - 1)
                    done.then_inc(mid_done, 1)
                    for f in range(8):
                        a = f // 2
                        pe.wait_ge(p_lo_done, after(8 * n + max(f - 1, 0)))
                        for t in range(2):
                            for k in range(CC):
                                at = slice(a * QUART + (f % 2 * 2 + t) * P, a * QUART + (f % 2 * 2 + t + 1) * P)
                                done = mm3(nc, ps_p[f % 2][:, t, :], fold_hi[:, k, at], fold_lo[:, k, at],
                                           cw_hi[:, a // 2, k, :], cw_lo[:, a // 2, k, :], k == 0, k == CC - 1)
                        done.then_inc(p_done, 1)
                    for c in range(CC):
                        m = 2 * n + c
                        ch = slice(c * P, (c + 1) * P)
                        pe.wait_ge(p_lo_done, after(8 * n + 8))
                        pe.wait_ge(mid_copied, after(2 * n + 2))
                        for a in (0, 2, 1, 3):
                            if c and a == 0:
                                pe.wait_ge(combined, after(2 * m - 1))
                                pe.wait_ge(sine_copied, after(2 * m - 1))
                            elif a == 1 or a == 0:
                                pe.wait_ge(combined, after(2 * m))
                                pe.wait_ge(sine_copied, after(2 * m))
                            for t in range(QT):
                                done = mm3(nc, ps_y[a][:], p_hi[a][:, t, ch], p_lo[a][:, t, ch], tab_hi[a][:, t, :], tab_lo[a][:, t, :],
                                           t == 0, t == QT - 1 and a != 0)
                            if a == 0:
                                done = nc.tensor.matmul(ps_y[0][:], mid[0:1, ch], sign_row[0:1, :], start=False, stop=True)
                            done.then_inc(y_done, 1)
                        pe.wait_ge(top_copied, after(m))
                        for t in range(QT):
                            nc.tensor.matmul(ps_w[1][:, 0, 0:2], p_hi[0][:, t, ch], sign_cols[:, t, :], start=t == 0, stop=False)
                            nc.tensor.matmul(ps_w[1][:, 0, 0:2], p_lo[0][:, t, ch], sign_cols[:, t, :], start=False, stop=False)
                        nc.tensor.matmul(ps_w[1][:, 0, 0:2], mid[0:1, ch], sign_row[0:1, 0:3:2], start=False, stop=True
                                         ).then_inc(top_done, 1)


def output(nc, ident, x_rows, row_code, col_code, w_out, o_rows, gate_rows_a, y_f, gate_row, hgrn_cols_in, final_norm_w, out_rows):
    KO = MIX // P
    H = D // 2
    with Room(nc, "out") as r:
        w_hi = r.sb("w_hi", [P, KO, D], F32R)
        w_lo = r.sb("w_lo", [P, KO, D], F32R)
        hn = r.sb("hn", [P, HEADS])
        eps = r.sb("eps", [P, 1])
        res_gate = r.sb("res_gate", [P, D])
        fnw = r.sb("fnw", [P, D])
        col = r.sb("col", [P, H])
        w_view = w_out[0].rearrange("(k p) n -> k p n", p=P)
        SMALL = P // GRID_W + 3
        W_ORDER = [*range(KT, KO), *range(KT)]
        w_hi_done, w_lo_done, small_here, eps_set = (r.sem(n) for n in ("w_hi_done", "w_lo_done", "small_here", "eps_set"))
        o = [[r.sb(f"o{d}{b}", [P, D]) for b in range(2)] for d in range(2)]
        ga = [r.sb(f"ga{b}", [P, D]) for b in range(2)]
        x = [r.sb(f"x{b}", [P, D]) for b in range(2)]
        row = r.sb("row", [P, H])
        yf = r.sb("yf", [P, KT, P])
        work = r.sb("work", [P, D])
        y_hi, y_lo = [r.sb(f"y_hi{i}", [P, KT, P], F32R) for i in range(2)], [r.sb(f"y_lo{i}", [P, KT, P], F32R) for i in range(2)]
        tmp = r.sb("tmp", [P, D])
        stat = r.sb("stat", [P, 3, HEADS])
        fin = r.sb("fin", [P, 3])
        ps_t = [r.ps(f"ps_t{i}", [P, KT // 2, P]) for i in range(2)]
        ps_o = [[r.ps(f"ps_o{b}{i}") for i in range(2)] for b in range(2)]
        o_here, x_here, out_stored, products_used = ([r.sem(f"{n}{b}") for b in range(2)] for n in
                                                     ("o_here", "x_here", "out_stored", "products_used"))
        (yf_here, summed, coded, squared, reduced, rooted, inverted, scaled, gated, turned, staged, f_hi, f_lo, a_hi, a_lo,
         f_half, a_half, residual, row_squared, row_rooted, row_inverted, finished, tmp_done) = (r.sem(n) for n in (
             "yf_here", "summed", "coded", "squared", "reduced", "rooted", "inverted", "scaled", "gated", "turned", "staged",
             "f_hi", "f_lo", "a_hi", "a_lo", "f_half", "a_half", "residual", "row_squared", "row_rooted", "row_inverted",
             "finished", "tmp_done"))
        w_raw = [r.sb("w_raw", [P, D]), tmp, ga[1], o[1][1]]
        RING = len(w_raw)
        w_here = [r.sem(f"w_here{n}", from_zero=True) for n in range(RING)]
        by_head = lambda ap: ap.rearrange("p (h n) -> p h n", h=HEADS)
        r.start_at_one()
        with nc.Block() as block:

            @block.gpsimd
            def _(pool):
                pool.memset(eps[:], EPS).then_inc(eps_set, 1)
                for n, k in enumerate(W_ORDER):
                    if n >= RING:
                        pool.wait_ge(w_lo_done, after(n - RING + 1))
                    pool.dma_start(w_raw[n % RING][:], w_view[k]).then_inc(w_here[n % RING], DMA)

            @block.sync
            def _(sp):
                with sp.Fori(0, NT // 2) as i:
                    for b in range(2):
                        t = 2 * i + b
                        tok = bass.ds(sp.snap(t * P), P)
                        codes = [bass.ds(sp.snap(t * 2 + half), 1) for half in range(2)]
                        if b == 1:
                            sp.wait_ge(w_lo_done, KO + 1)
                        sp.wait_ge(turned, after(2 * i))
                        for d in range(2):
                            sp.dma_start(o[d][b][:], o_rows[d][tok, :]).then_inc(o_here[b], DMA)
                        sp.dma_start(ga[b][:], gate_rows_a[tok, :]).then_inc(o_here[b], DMA)
                        sp.wait_ge(out_stored[b], after(i * DMA))
                        sp.dma_start(x[b][:], x_rows[tok, :]).then_inc(x_here[b], DMA)
                        sp.wait_ge(coded, after(t))
                        for half in range(2):
                            sp.dma_start(row[half * GRID_W:(half + 1) * GRID_W, :],
                                         row_code[codes[half], :].to_broadcast([GRID_W, H])).then_inc(x_here[b], DMA)
                        sp.wait_ge(yf_here, 1)
                        sp.wait_ge(f_lo, after(t))
                        sp.dma_start(yf[:], y_f[:, tok].rearrange("(k p) t -> p k t", p=P)).then_inc(yf_here, DMA)

            @block.vector
            def _(v):
                def front(i, b):
                    t = 2 * i + b
                    oo = o[0][b]
                    v.wait_ge(o_here[b], after((i + 1) * 3 * DMA))
                    nc.vector.tensor_tensor(oo[:], oo[:], o[1][b][:], ALU.add).then_inc(summed, 1)
                    v.wait_ge(x_here[b], after((i + 1) * 3 * DMA))
                    nc.vector.tensor_tensor(x[b][:, 0:H], x[b][:, 0:H], row[:], ALU.add)
                    nc.vector.tensor_tensor(x[b][:, H:D], x[b][:, H:D], col[:], ALU.add).then_inc(coded, 1)
                    v.wait_ge(squared, after(t + 1))
                    nc.vector.tensor_reduce(stat[:, 0, :], by_head(work[:]), AX.X, ALU.add).then_inc(reduced, 1)
                    v.wait_ge(yf_here, after((t + 1) * DMA))
                    v.wait_ge(f_half, after(t))
                    nc.vector.tensor_copy(y_hi[1][:], yf[:]).then_inc(f_hi, 1)
                    v.wait_ge(rooted, after(t + 1))
                    nc.vector.reciprocal(stat[:, 2, :], stat[:, 1, :]).then_inc(inverted, 1)
                    v.wait_ge(f_hi, after(t + 1))
                    nc.vector.tensor_tensor(y_lo[1][:], yf[:], y_hi[1][:].bitcast(F32), ALU.subtract).then_inc(f_lo, 1)
                    v.wait_ge(inverted, after(t + 1))
                    inv = stat[:, 2, :].rearrange("p (h o) -> p h o", o=1).to_broadcast([P, HEADS, P])
                    nc.vector.tensor_tensor(by_head(oo[:]), by_head(oo[:]), inv, ALU.mult).then_inc(scaled, 1)
                    v.wait_ge(scaled, after(t + 1))
                    nc.vector.tensor_tensor(oo[:], oo[:], ga[b][:], ALU.mult).then_inc(gated, 1)

                def split_heads(t):
                    v.wait_ge(staged, after(t + 1))
                    v.wait_ge(a_half, after(t))
                    nc.vector.tensor_copy(y_hi[0][:], work[:].rearrange("p (k n) -> p k n", k=KT)).then_inc(a_hi, 1)
                    v.wait_ge(a_hi, after(t + 1))
                    nc.vector.tensor_tensor(y_lo[0][:], work[:].rearrange("p (k n) -> p k n", k=KT), y_hi[0][:].bitcast(F32),
                                            ALU.subtract).then_inc(a_lo, 1)

                def finish(i, b):
                    t = 2 * i + b
                    v.wait_ge(a_half, after(t + 1))
                    v.wait_ge(row_squared, after(t))
                    for j in range(2):
                        cols = slice(j * H, (j + 1) * H)
                        last = nc.vector.tensor_tensor(tmp[:, cols], ps_o[b][j][:], res_gate[:, cols], ALU.mult)
                    last.then_inc(products_used[b], 1)
                    v.wait_ge(products_used[b], after(i + 1))
                    nc.vector.tensor_tensor(x[b][:], x[b][:], tmp[:], ALU.add).then_inc(residual, 1)
                    v.wait_ge(row_rooted, after(t + 1))
                    nc.vector.reciprocal(fin[:, 2:3], fin[:, 1:2]).then_inc(row_inverted, 1)
                    v.wait_ge(row_inverted, after(t + 1))
                    nc.vector.scalar_tensor_tensor(x[b][:], x[b][:], fin[:, 2:3], fnw[:], ALU.mult, ALU.mult).then_inc(finished, 1)

                def turn(i, last):
                    front(i, 1)
                    split_heads(2 * i + 1)
                    finish(i, 0)
                    if not last:
                        front(i + 1, 0)
                        split_heads(2 * i + 2)
                    finish(i, 1)

                def split_weights_low(ns):
                    for n in ns:
                        k = W_ORDER[n]
                        v.wait_ge(w_hi_done, after(n + 1))
                        nc.vector.tensor_tensor(w_lo[:, k, :], w_raw[n % RING][:], w_hi[:, k, :].bitcast(F32),
                                                ALU.subtract).then_inc(w_lo_done, 1)

                split_weights_low(range(KT))
                v.wait_ge(small_here, after(SMALL * DMA))
                front(0, 0)
                split_heads(0)
                split_weights_low(range(KT, KO))
                with v.Fori(0, NT // 2 - 1) as i:
                    turn(i, False)
                turn(NT // 2 - 1, True)

            @block.scalar
            def _(act):
                def front(i, b):
                    t = 2 * i + b
                    act.wait_ge(summed, after(t + 1))
                    act.wait_ge(a_lo, after(t))
                    nc.scalar.activation(work[:], o[0][b][:], ACT.Square).then_inc(squared, 1)
                    act.wait_ge(reduced, after(t + 1))
                    nc.scalar.activation(stat[:, 1, :], stat[:, 0, :], ACT.Sqrt, scale=1.0 / P, bias=eps[:, 0:1]).then_inc(rooted, 1)

                def stage_heads(t):
                    act.wait_ge(turned, after(t + 1))
                    for k in range(KT):
                        last = nc.scalar.activation(work[:, k * P:(k + 1) * P], ps_t[k // 4][:, k % 4, :], ACT.Copy, scale=hn[:, k:k + 1])
                    last.then_inc(staged, 1)

                def finish(i, b):
                    t = 2 * i + b
                    act.wait_ge(residual, after(t + 1))
                    nc.scalar.activation(tmp[:], x[b][:], ACT.Square, accum_out=fin[:, 0:1]).then_inc(row_squared, 1)
                    act.wait_ge(row_squared, after(t + 1))
                    nc.scalar.activation(fin[:, 1:2], fin[:, 0:1], ACT.Sqrt, scale=1.0 / D, bias=eps[:, 0:1]).then_inc(row_rooted, 1)
                    act.wait_ge(finished, after(t + 1))
                    act.dma_start(out_rows[bass.ds(t * P, P), :], x[b][:]).then_inc(out_stored[b], DMA)

                def turn(i, last):
                    front(i, 1)
                    stage_heads(2 * i + 1)
                    finish(i, 0)
                    if not last:
                        front(i + 1, 0)
                        stage_heads(2 * i + 2)
                    finish(i, 1)

                def split_weights_high(ns):
                    for n in ns:
                        act.wait_ge(w_here[n % RING], (n // RING + 1) * DMA)
                        nc.scalar.activation(w_hi[:, W_ORDER[n], :], w_raw[n % RING][:], ACT.Copy).then_inc(w_hi_done, 1)

                for i in range(P // GRID_W):
                    act.dma_start(col[i * GRID_W:(i + 1) * GRID_W, :], col_code).then_inc(small_here, DMA)
                act.dma_start(hn[:], hgrn_cols_in).then_inc(small_here, DMA)
                act.dma_start(res_gate[:], row_on_all(gate_row[0, :], D)).then_inc(small_here, DMA)
                act.dma_start(fnw[:], row_on_all(final_norm_w, D)).then_inc(small_here, DMA)
                act.wait_ge(eps_set, after(1))
                split_weights_high(range(KT))
                act.wait_ge(small_here, after(SMALL * DMA))
                front(0, 0)
                stage_heads(0)
                split_weights_high(range(KT, KO))
                with act.Fori(0, NT // 2 - 1) as i:
                    turn(i, False)
                turn(NT // 2 - 1, True)
                for b in range(2):
                    act.wait_ge(out_stored[b], after(NT // 2 * DMA))

            @block.tensor
            def _(pe):
                def transpose_heads(t, b):
                    pe.wait_ge(gated, after(t + 1))
                    pe.wait_ge(staged, after(t))
                    for k in range(KT):
                        last = nc.tensor.transpose(ps_t[k // 4][:, k % 4, :], o[0][b][:, k * P:(k + 1) * P], ident[:])
                    last.then_inc(turned, 1)

                def project(i, b, weights_arrive=False):
                    t = 2 * i + b
                    pe.wait_ge(products_used[b], after(i))
                    for part, split, signal in ((1, f_lo, f_half), (0, a_lo, a_half)):
                        pe.wait_ge(split, after(t + 1))
                        for k in range(KT):
                            if weights_arrive:
                                pe.wait_ge(w_lo_done, after(W_ORDER.index(part * KT + k) + 1))
                            for j in range(2):
                                ko, cols = part * KT + k, slice(j * H, (j + 1) * H)
                                last = mm3(nc, ps_o[b][j][:], y_hi[part][:, k, :], y_lo[part][:, k, :], w_hi[:, ko, cols], w_lo[:, ko, cols],
                                           part == 1 and k == 0, part == 0 and k == KT - 1)
                        last.then_inc(signal, 1)

                def turn(i, last, first=False):
                    project(i, 0, first)
                    transpose_heads(2 * i + 1, 1)
                    project(i, 1)
                    if not last:
                        transpose_heads(2 * i + 2, 0)

                transpose_heads(0, 0)
                turn(0, False, True)
                with pe.Fori(1, NT // 2 - 1) as i:
                    turn(i, False)
                turn(NT // 2 - 1, True)


def program(nc, x, ctx, w_ada, b_ada, w_in, w_fourier, w_out, final_norm_w, conds, b_ada_cols, norm_w_cols, bounds_cols,
            hgrn_cols, b_fourier_cols, row_code, col_code, masks_in, tables, chan_tables, sign_cols, sign_row, out):
    def scratch(name, shape):
        return nc.dram_tensor(name, shape, F32).ap()

    gate_row = scratch("residual_gate", (1, D))
    states = [scratch(f"context_state{d}", (HG, P)) for d in range(2)]
    value_rows, gate_rows_a = scratch("value_rows", (SEQ, HG)), scratch("gate_rows_a", (SEQ, HG))
    o_rows = [scratch(f"head_out{d}", (SEQ, HG)) for d in range(2)]
    pieces = {name: scratch(f"piece_{name}", (HG, SEQ)) for name in PIECES}
    y_f = scratch("fourier_out", (FW, SEQ))
    with Room(nc, "all") as r:
        ident = r.sb("ident", [P, P])
        with Room(nc, "hidden") as s:
            masks = s.sb("masks", [P, 2, MASKED, P], U8)
            mod_mul, mod_add = s.sb("mod_mul", [P, KT, 2]), s.sb("mod_add", [P, KT, 2])
            one_minus_lb = s.sb("one_minus_lb", [P, 2, HEADS])
            constants(nc, masks_in, ident, masks)
            modulation(nc, conds, w_ada, b_ada, b_ada_cols, norm_w_cols, bounds_cols, ident, mod_mul, mod_add, one_minus_lb, gate_row)
            with Room(nc, "c") as t:
                hi, lo = t.sb("h_hi", [P, KT, CTX], F32R), t.sb("h_lo", [P, KT, CTX], F32R)
                hidden(nc, "hc", ctx[0], CTX // P, 1, None, None, mod_mul, mod_add, ident, hi, lo)
                context(nc, w_in, one_minus_lb, ident, hi, lo, states)
            with Room(nc, "x") as t:
                hi, lo = t.sb("h_hi", [P, KT, SEQ], F32R), t.sb("h_lo", [P, KT, SEQ], F32R)
                hidden(nc, "hx", x[0], NT, 0, row_code, col_code, mod_mul, mod_add, ident, hi, lo)
                natural(nc, w_in, hi, lo, value_rows, gate_rows_a)
                first_head(nc, w_in, hi, lo, pieces)
                heads(nc, w_in, one_minus_lb, ident, masks, hi, lo, states, value_rows, pieces, o_rows)
        fourier(nc, tables, chan_tables, sign_cols, sign_row, w_fourier[0].rearrange("g c d -> (g c) d"), b_fourier_cols,
                pieces["wave"], pieces["gate_f"], y_f)
        output(nc, ident, x[0], row_code, col_code, w_out, o_rows, gate_rows_a, y_f, gate_row, hgrn_cols, final_norm_w, out[0])


def as_columns(v):
    return np.ascontiguousarray(np.asarray(v).reshape(-1, P).T)


def position_codes():
    quarter = D // 4
    omega = np.power(np.float32(10000.0), -np.arange(quarter, dtype=np.float32) / np.float32(quarter))

    def code(n):
        angle = (np.arange(n, dtype=np.float32)[:, None] * omega[None, :]).astype(np.float64)
        return np.concatenate([np.sin(angle), np.cos(angle)], axis=-1).astype(np.float32)

    return code(SEQ // GRID_W), code(GRID_W)


AS_GIVEN = ["x", "ctx", "w_ada", "b_ada", "w_in", "w_fourier", "w_out", "final_norm_w"]


def kernel(**inputs):
    import concourse.bacc as bacc
    from concourse.bass_utils import run_bass_kernel_spmd

    nc = bacc.Bacc("TRN2", target_bir_lowering=False, num_devices=1)
    row_code, col_code = position_codes()
    tables, chan_tables, sign_cols, sign_row = wave_tables()
    given = {name: inputs[name] for name in AS_GIVEN}
    given |= {
        "conds": np.stack([as_columns(inputs["c"]), as_columns(inputs["c_ctx"])], axis=-1),
        "b_ada_cols": as_columns(inputs["b_ada"]),
        "norm_w_cols": as_columns(inputs["norm_w"]),
        "bounds_cols": as_columns(inputs["lower_bounds"]).reshape(P, 2, HEADS),
        "hgrn_cols": as_columns(inputs["hgrn_norm_w"]),
        "b_fourier_cols": as_columns(inputs["b_fourier"]),
        "row_code": row_code, "col_code": col_code, "masks": score_masks(),
        "tables": tables, "chan_tables": chan_tables, "sign_cols": sign_cols, "sign_row": sign_row,
    }
    arrays, args = {}, []
    for name, a in given.items():
        a = np.ascontiguousarray(a)
        arrays[f"in_{name}"] = a
        args.append(nc.dram_tensor(f"in_{name}", a.shape, mybir.dt.from_np(a.dtype), kind="ExternalInput").ap())
    args.append(nc.dram_tensor("out", (1, SEQ, D), F32, kind="ExternalOutput").ap())
    program(nc, *args)
    return run_bass_kernel_spmd(nc, [arrays], core_ids=[0]).results[0]["out"]
```
